# Optimizing a Trainium2 kernel written in Bass

```python
import math
import jax
import jax.numpy as jnp
from jax import lax
import numpy as np

D_MODEL = 1024
BATCH = 1
SEQ = 256
DEPTH = 1
DEC_BATCH = 8
DEC_SEQ = 1
PAST_LEN = 256
PAGE_SIZE = 128

HEAD_DIM = 64
N_HEADS = D_MODEL // HEAD_DIM
ATTN_WIDTH = N_HEADS * HEAD_DIM
ROT_DIM = HEAD_DIM // 4
ROPE_THETA = 500000.0
MOBA_BLOCK = 256
MOBA_TOPK = 3
Q_CHUNK = 64
SSM_HEAD_DIM = 64
SSM_WIDTH = D_MODEL
SSM_HEADS = SSM_WIDTH // SSM_HEAD_DIM
SSM_GROUPS = 2
D_STATE = 128
CONV_W = 4
SSD_CHUNK = 128
CONV_DIM = SSM_WIDTH + 2 * SSM_GROUPS * D_STATE
MIX_WIDTH = ATTN_WIDTH + SSM_WIDTH
IN_COLS = 3 * ATTN_WIDTH + SSM_WIDTH + CONV_DIM + SSM_HEADS
PEER_HEADS = 8
PEER_NKEYS = 128
PEER_EXPERTS = PEER_NKEYS * PEER_NKEYS
PEER_QDIM = 256
PEER_TOPK = 16
PEER_CHUNK = 256
EPS = 1e-6
NEG_INF = -1e30

kernel_name = 'hybrid_moba_ssd_peer_step'

def _rms(x):
    xf = x.astype(jnp.float32)
    y = xf * lax.rsqrt(jnp.mean(xf * xf, axis=-1, keepdims=True) + EPS)
    return y.astype(x.dtype)

def rmsnorm(x, g):
    return _rms(x) * g

def apply_partial_rope(x, pos):
    half = ROT_DIM // 2
    inv_freq = ROPE_THETA ** (-jnp.arange(half, dtype=jnp.float32) / half)
    ang = pos.astype(jnp.float32)[:, None] * inv_freq[None, :]
    cos = jnp.cos(ang)[:, None, :]
    sin = jnp.sin(ang)[:, None, :]
    xr = x[..., :ROT_DIM].astype(jnp.float32)
    x1, x2 = xr[..., :half], xr[..., half:]
    rot = jnp.concatenate([x1 * cos - x2 * sin, x2 * cos + x1 * sin], axis=-1).astype(x.dtype)
    return jnp.concatenate([rot, x[..., ROT_DIM:]], axis=-1)

def dense_fetch(rows):
    n = rows.shape[0]
    def fetch(pos):
        h = jnp.arange(N_HEADS).reshape((N_HEADS,) + (1,) * (pos.ndim - 1))
        return rows[jnp.clip(pos, 0, n - 1), h]
    return fetch

def paged_fetch(pool, new, pt_row, past_len):
    n_pages = pt_row.shape[0]
    t_new = new.shape[0]
    def fetch(pos):
        h = jnp.arange(N_HEADS).reshape((N_HEADS,) + (1,) * (pos.ndim - 1))
        phys = pt_row[jnp.clip(pos // PAGE_SIZE, 0, n_pages - 1)]
        r_past = pool[phys, pos % PAGE_SIZE, h]
        r_new = new[jnp.clip(pos - past_len, 0, t_new - 1), h]
        return jnp.where((pos < past_len)[..., None], r_past, r_new)
    return fetch

def moba_core(q, q_pos, means, fetch_k, fetch_v):
    nh, nq, _ = q.shape
    nb = means.shape[1]
    ksel = min(MOBA_TOPK, nb)
    q_blk = q_pos // MOBA_BLOCK
    gate = jnp.einsum('hqd,hnd->hqn', q, means).astype(jnp.float32)
    gate = jnp.where(jnp.arange(nb)[None, :] < q_blk[:, None], gate, NEG_INF)
    _, idx = lax.top_k(gate, ksel)
    sel_ok = idx < q_blk[:, None]
    offs = jnp.arange(MOBA_BLOCK, dtype=jnp.int32)
    sel_pos = idx[..., None] * MOBA_BLOCK + offs
    own_pos = jnp.broadcast_to((q_blk * MOBA_BLOCK)[:, None] + offs, (nh, nq, MOBA_BLOCK))
    k_sel, v_sel = fetch_k(sel_pos), fetch_v(sel_pos)
    k_own, v_own = fetch_k(own_pos), fetch_v(own_pos)
    scale = HEAD_DIM ** -0.5
    s_sel = jnp.einsum('hqd,hqjtd->hqjt', q, k_sel).astype(jnp.float32) * scale
    s_sel = jnp.where(sel_ok[..., None], s_sel, NEG_INF).reshape(nh, nq, ksel * MOBA_BLOCK)
    s_own = jnp.einsum('hqd,hqtd->hqt', q, k_own).astype(jnp.float32) * scale
    s_own = jnp.where(own_pos <= q_pos[:, None], s_own, NEG_INF)
    p = jax.nn.softmax(jnp.concatenate([s_sel, s_own], axis=-1), axis=-1).astype(v_own.dtype)
    p_sel = p[..., :ksel * MOBA_BLOCK].reshape(nh, nq, ksel, MOBA_BLOCK)
    p_own = p[..., ksel * MOBA_BLOCK:]
    return (jnp.einsum('hqjt,hqjtd->hqd', p_sel, v_sel)
            + jnp.einsum('hqt,hqtd->hqd', p_own, v_own))

def moba_prompt(q, k, v):
    bn, s = q.shape[:2]
    nb = -(-s // MOBA_BLOCK)
    kp = jnp.pad(k.astype(jnp.float32), ((0, 0), (0, nb * MOBA_BLOCK - s), (0, 0), (0, 0)))
    means = kp.reshape(bn, nb, MOBA_BLOCK, N_HEADS, HEAD_DIM).mean(axis=2)
    means = means.transpose(0, 2, 1, 3).astype(q.dtype)
    nq = s // Q_CHUNK
    pc = jnp.arange(s, dtype=jnp.int32).reshape(nq, Q_CHUNK)

    def one_seq(args):
        q1, k1, v1, m1 = args
        fk, fv = dense_fetch(k1), dense_fetch(v1)
        qc = q1.reshape(nq, Q_CHUNK, N_HEADS, HEAD_DIM).transpose(0, 2, 1, 3)
        o = lax.map(lambda a: moba_core(a[0], a[1], m1, fk, fv), (qc, pc))
        return o.transpose(0, 2, 1, 3).reshape(s, ATTN_WIDTH)

    return lax.map(one_seq, (q, k, v, means))

def moba_sample(q, k, v, pool_k, pool_v, page_table):
    bn, t = q.shape[:2]
    n_pages = page_table.shape[1]
    past = n_pages * PAGE_SIZE
    nb = -(-(past + t) // MOBA_BLOCK)
    ppb = MOBA_BLOCK // PAGE_SIZE
    n_new_pages = -(-t // PAGE_SIZE)
    page_sums = pool_k.astype(jnp.float32).sum(axis=1)[page_table]
    kn = jnp.pad(k.astype(jnp.float32), ((0, 0), (0, n_new_pages * PAGE_SIZE - t), (0, 0), (0, 0)))
    new_sums = kn.reshape(bn, n_new_pages, PAGE_SIZE, N_HEADS, HEAD_DIM).sum(axis=2)
    sums = jnp.concatenate([page_sums, new_sums], axis=1)
    sums = jnp.pad(sums, ((0, 0), (0, nb * ppb - sums.shape[1]), (0, 0), (0, 0)))
    means = sums.reshape(bn, nb, ppb, N_HEADS, HEAD_DIM).sum(axis=2) / MOBA_BLOCK
    means = means.transpose(0, 2, 1, 3).astype(q.dtype)
    q_pos = past + jnp.arange(t, dtype=jnp.int32)

    def one_seq(args):
        q1, k1, v1, m1, pt = args
        fk = paged_fetch(pool_k, k1, pt, past)
        fv = paged_fetch(pool_v, v1, pt, past)
        o = moba_core(q1.transpose(1, 0, 2), q_pos, m1, fk, fv)
        return o.transpose(1, 0, 2).reshape(t, ATTN_WIDTH)

    return lax.map(one_seq, (q, k, v, means, page_table))

def causal_conv(xbc, conv_state, w, b):
    xp = jnp.concatenate([conv_state.astype(xbc.dtype), xbc], axis=1)
    y = lax.conv_general_dilated(xp, w[:, None, :].astype(xbc.dtype), window_strides=(1,),
                                 padding='VALID', dimension_numbers=('NWC', 'WIO', 'NWC'),
                                 feature_group_count=CONV_DIM)
    return jax.nn.silu(y + b), xp[:, xp.shape[1] - (CONV_W - 1):]

def ssd_scan(x, dt, a, b_in, c_in, h0):
    bn, l = x.shape[:2]
    q = min(SSD_CHUNK, l)
    nc = -(-l // q)
    pad = nc * q - l
    hg = SSM_HEADS // SSM_GROUPS

    def blocks(t, tail):
        t = jnp.pad(t, ((0, 0), (0, pad)) + ((0, 0),) * (t.ndim - 2))
        return jnp.moveaxis(t.reshape((bn, nc, q) + tail), 1, 0)

    xc = blocks(x.astype(jnp.float32), (SSM_GROUPS, hg, SSM_HEAD_DIM))
    dtc = blocks(dt, (SSM_GROUPS, hg))
    bc = blocks(b_in.astype(jnp.float32), (SSM_GROUPS, D_STATE))
    cc = blocks(c_in.astype(jnp.float32), (SSM_GROUPS, D_STATE))
    ag = a.reshape(SSM_GROUPS, hg)
    causal = jnp.tril(jnp.ones((q, q), dtype=bool))[None, :, :, None, None]

    def step(h, inp):
        xq, dq, bq, cq = inp
        acs = jnp.cumsum(dq * ag, axis=1)
        seg = acs[:, :, None] - acs[:, None, :]
        decay = jnp.exp(jnp.where(causal, seg, -jnp.inf))
        cb = jnp.einsum('btgn,bsgn->btsg', cq, bq)
        w = cb[..., None] * decay * dq[:, None]
        y = jnp.einsum('btsgh,bsghp->btghp', w, xq)
        y = y + jnp.einsum('btgn,bghpn->btghp', cq, h) * jnp.exp(acs)[..., None]
        to_end = jnp.exp(acs[:, -1:] - acs) * dq
        h = (h * jnp.exp(acs[:, -1])[..., None, None]
             + jnp.einsum('bsgn,bsgh,bsghp->bghpn', bq, to_end, xq))
        return h, y

    h0g = h0.astype(jnp.float32).reshape(bn, SSM_GROUPS, hg, SSM_HEAD_DIM, D_STATE)
    h_t, y = lax.scan(step, h0g, (xc, dtc, bc, cc))
    y = jnp.moveaxis(y, 0, 1).reshape(bn, nc * q, SSM_HEADS, SSM_HEAD_DIM)[:, :l]
    return y, h_t.reshape(bn, SSM_HEADS, SSM_HEAD_DIM, D_STATE)

def token_mix(xn, pos, attend, conv_state, ssm_state, w_in, conv_w, conv_b, dt_bias, a_log,
              d_skip, g_attn, g_ssd, w_out):
    bn, l, _ = xn.shape
    proj = xn @ w_in
    q, k, v, z, xbc, dt_raw = jnp.split(
        proj, [ATTN_WIDTH, 2 * ATTN_WIDTH, 3 * ATTN_WIDTH, 3 * ATTN_WIDTH + SSM_WIDTH,
               3 * ATTN_WIDTH + SSM_WIDTH + CONV_DIM], axis=-1)
    heads = (bn, l, N_HEADS, HEAD_DIM)
    q = apply_partial_rope(q.reshape(heads), pos)
    k = apply_partial_rope(k.reshape(heads), pos)
    v = v.reshape(heads)
    attn = rmsnorm(attend(q, k, v), g_attn)
    xbc, conv_new = causal_conv(xbc, conv_state, conv_w, conv_b)
    xs, b_in, c_in = jnp.split(xbc, [SSM_WIDTH, SSM_WIDTH + SSM_GROUPS * D_STATE], axis=-1)
    xs = xs.reshape(bn, l, SSM_HEADS, SSM_HEAD_DIM)
    dt = jax.nn.softplus(dt_raw.astype(jnp.float32) + dt_bias.astype(jnp.float32))
    a = -jnp.exp(a_log.astype(jnp.float32))
    y, ssm_new = ssd_scan(xs, dt, a, b_in.reshape(bn, l, SSM_GROUPS, D_STATE),
                          c_in.reshape(bn, l, SSM_GROUPS, D_STATE), ssm_state)
    y = (y + d_skip.astype(jnp.float32)[:, None] * xs.astype(jnp.float32))
    y = y.reshape(bn, l, SSM_WIDTH).astype(xn.dtype) * jax.nn.silu(z)
    y = _rms(y.reshape(bn, l, SSM_GROUPS, SSM_WIDTH // SSM_GROUPS)).reshape(bn, l, SSM_WIDTH) * g_ssd
    out = jnp.concatenate([attn, y], axis=-1) @ w_out
    return out, k, v, conv_new, ssm_new.astype(xn.dtype)

def peer_ffn(xn, wq, sub_keys, u_emb, v_emb):
    bn, l, d = xn.shape
    t = bn * l
    c = min(PEER_CHUNK, t)
    nc = -(-t // c)
    x2 = jnp.pad(xn.reshape(t, d), ((0, nc * c - t), (0, 0))).reshape(nc, c, d)

    def chunk(xb):
        qh = (xb @ wq).reshape(c, PEER_HEADS, 2, PEER_QDIM // 2)
        s = jnp.einsum('chid,hikd->chik', qh, sub_keys).astype(jnp.float32)
        sv, si = lax.top_k(s, PEER_TOPK)
        cand = (sv[:, :, 0, :, None] + sv[:, :, 1, None, :]).reshape(c, PEER_HEADS, PEER_TOPK * PEER_TOPK)
        best, bi = lax.top_k(cand, PEER_TOPK)
        i1 = jnp.take_along_axis(si[:, :, 0], bi // PEER_TOPK, axis=-1)
        i2 = jnp.take_along_axis(si[:, :, 1], bi % PEER_TOPK, axis=-1)
        e = i1 * PEER_NKEYS + i2
        g = jax.nn.softmax(best, axis=-1).astype(xb.dtype)
        act = jax.nn.gelu(jnp.einsum('cd,chkd->chk', xb, u_emb[e]), approximate=False)
        return jnp.einsum('chk,chkd->cd', g * act, v_emb[e])

    out = lax.map(chunk, x2).reshape(nc * c, d)[:t]
    return out.reshape(bn, l, d)

def setup_inputs(seed: int = 0) -> dict:
    key = jax.random.key(seed)
    ks = jax.random.split(key, 24)
    f32 = jnp.float32

    def nrm(k, shape, s):
        return jax.random.normal(k, shape, f32) * s

    n_pages = PAST_LEN // PAGE_SIZE
    n_used = DEC_BATCH * n_pages
    n_pool = n_used + max(1, n_used // 4)
    x_prompt = nrm(ks[0], (BATCH, SEQ, D_MODEL), 1.0)
    x_sample = nrm(ks[1], (DEC_BATCH, DEC_SEQ, D_MODEL), 1.0)
    cache_k = nrm(ks[2], (DEPTH, n_pool, PAGE_SIZE, N_HEADS, HEAD_DIM), 1.0)
    cache_v = nrm(ks[3], (DEPTH, n_pool, PAGE_SIZE, N_HEADS, HEAD_DIM), 1.0)
    perm = jax.random.permutation(ks[4], n_pool)
    page_table = perm[:n_used].reshape(DEC_BATCH, n_pages).astype(jnp.int32)
    state_conv = nrm(ks[5], (DEPTH, DEC_BATCH, CONV_W - 1, CONV_DIM), 1.0)
    state_ssm = nrm(ks[6], (DEPTH, DEC_BATCH, SSM_HEADS, SSM_HEAD_DIM, D_STATE), 0.1)
    g_mix = 1.0 + nrm(ks[7], (DEPTH, D_MODEL), 0.02)
    w_in = nrm(ks[8], (DEPTH, D_MODEL, IN_COLS), D_MODEL ** -0.5)
    conv_w = nrm(ks[9], (DEPTH, CONV_W, CONV_DIM), CONV_W ** -0.5)
    conv_b = nrm(ks[10], (DEPTH, CONV_DIM), 0.02)
    dt0 = jnp.exp(jax.random.uniform(ks[11], (DEPTH, SSM_HEADS), f32, math.log(1e-3), math.log(1e-1)))
    dt_bias = dt0 + jnp.log(-jnp.expm1(-dt0))
    a_log = jnp.log(jax.random.uniform(ks[12], (DEPTH, SSM_HEADS), f32, 1.0, 16.0))
    d_skip = 1.0 + nrm(ks[13], (DEPTH, SSM_HEADS), 0.1)
    g_attn = 1.0 + nrm(ks[14], (DEPTH, ATTN_WIDTH), 0.02)
    g_ssd = 1.0 + nrm(ks[15], (DEPTH, SSM_WIDTH), 0.02)
    w_out = nrm(ks[16], (DEPTH, MIX_WIDTH, D_MODEL), MIX_WIDTH ** -0.5)
    g_ffn = 1.0 + nrm(ks[17], (DEPTH, D_MODEL), 0.02)
    peer_wq = nrm(ks[18], (DEPTH, D_MODEL, PEER_HEADS * PEER_QDIM), D_MODEL ** -0.5)
    peer_keys = nrm(ks[19], (DEPTH, PEER_HEADS, 2, PEER_NKEYS, PEER_QDIM // 2), (PEER_QDIM // 2) ** -0.5)
    peer_u = nrm(ks[20], (DEPTH, PEER_EXPERTS, D_MODEL), D_MODEL ** -0.5)
    peer_v = nrm(ks[21], (DEPTH, PEER_EXPERTS, D_MODEL), PEER_HEADS ** -0.5)
    g_final = 1.0 + nrm(ks[22], (D_MODEL,), 0.02)
    return {'x_prompt': x_prompt, 'x_sample': x_sample, 'cache_k': cache_k, 'cache_v': cache_v,
            'page_table': page_table, 'state_conv': state_conv, 'state_ssm': state_ssm,
            'g_mix': g_mix, 'w_in': w_in, 'conv_w': conv_w, 'conv_b': conv_b, 'dt_bias': dt_bias,
            'a_log': a_log, 'd_skip': d_skip, 'g_attn': g_attn, 'g_ssd': g_ssd, 'w_out': w_out,
            'g_ffn': g_ffn, 'peer_wq': peer_wq, 'peer_keys': peer_keys, 'peer_u': peer_u,
            'peer_v': peer_v, 'g_final': g_final}

def reference(x_prompt, x_sample, cache_k, cache_v, page_table, state_conv, state_ssm,
              g_mix, w_in, conv_w, conv_b, dt_bias, a_log, d_skip, g_attn, g_ssd, w_out,
              g_ffn, peer_wq, peer_keys, peer_u, peer_v, g_final):
    pos_p = jnp.arange(x_prompt.shape[1], dtype=jnp.int32)
    pos_s = page_table.shape[1] * PAGE_SIZE + jnp.arange(x_sample.shape[1], dtype=jnp.int32)
    hp, hs = x_prompt, x_sample
    kp_l, vp_l, ks_l, vs_l, cp_l, cs_l, sp_l, ss_l = [], [], [], [], [], [], [], []
    for l in range(DEPTH):
        lw = (w_in[l], conv_w[l], conv_b[l], dt_bias[l], a_log[l], d_skip[l], g_attn[l], g_ssd[l], w_out[l])
        conv0 = jnp.zeros((hp.shape[0], CONV_W - 1, CONV_DIM), hp.dtype)
        ssm0 = jnp.zeros((hp.shape[0], SSM_HEADS, SSM_HEAD_DIM, D_STATE), hp.dtype)
        mp, kp, vp, cp, sp = token_mix(rmsnorm(hp, g_mix[l]), pos_p, moba_prompt, conv0, ssm0, *lw)
        attend_s = lambda q, k, v, l=l: moba_sample(q, k, v, cache_k[l], cache_v[l], page_table)
        ms, kk, vv, cs, ss = token_mix(rmsnorm(hs, g_mix[l]), pos_s, attend_s,
                                       state_conv[l], state_ssm[l], *lw)
        hp = hp + mp
        hs = hs + ms
        hp = hp + peer_ffn(rmsnorm(hp, g_ffn[l]), peer_wq[l], peer_keys[l], peer_u[l], peer_v[l])
        hs = hs + peer_ffn(rmsnorm(hs, g_ffn[l]), peer_wq[l], peer_keys[l], peer_u[l], peer_v[l])
        kp_l.append(kp)
        vp_l.append(vp)
        ks_l.append(kk)
        vs_l.append(vv)
        cp_l.append(cp)
        cs_l.append(cs)
        sp_l.append(sp)
        ss_l.append(ss)
    y_prompt = rmsnorm(hp, g_final)
    y_sample = rmsnorm(hs, g_final)
    k_prompt = jnp.stack(kp_l)
    v_prompt = jnp.stack(vp_l)
    k_sample = jnp.stack(ks_l)
    v_sample = jnp.stack(vs_l)
    conv_prompt = jnp.stack(cp_l)
    conv_sample = jnp.stack(cs_l)
    ssm_prompt = jnp.stack(sp_l)
    ssm_sample = jnp.stack(ss_l)
    return (y_prompt, y_sample, k_prompt, v_prompt, k_sample, v_sample, conv_prompt, conv_sample, ssm_prompt, ssm_sample)


_drawn_inputs = setup_inputs


def setup_inputs(seed=0):
    import zlib

    import numpy as np

    out = dict(_drawn_inputs(seed))
    spreads = {}
    factors = {'g_attn': 3.345, 'g_ffn': 2.95, 'g_final': 2.822}
    for name, (base, spread) in spreads.items():
        noise = np.random.default_rng([zlib.crc32(name.encode()), seed]).standard_normal(out[name].shape)
        drawn = base * np.exp(spread * noise) if base else spread * noise
        out[name] = jnp.asarray(drawn.astype(out[name].dtype))
    for name, factor in factors.items():
        out[name] = (out[name] * factor).astype(out[name].dtype)
    return out
```

```python
from contextlib import ExitStack

import numpy as np

import concourse.bass as bass
from concourse import mybir

ALU = mybir.AluOpType
ACT = mybir.ActivationFunctionType
F32 = mybir.dt.float32
U32 = mybir.dt.uint32
I32 = mybir.dt.int32
AX_X = mybir.AxisListType.X

P = 128
D = 1024
KD = D // P
TP = 256
NB = 8
NT = TP + NB
TT = TP // P
TILES = TT + 1
HD = 64
NH = 16
PAST = 256
PAGE = 128
NPG = PAST // PAGE
ROT = HD // 4
GROUPS = 2
CONV_W = 4
CONV_CH = 12
Q0, K0, V0, Z0, X0 = 0, KD, 2 * KD, 3 * KD, 4 * KD
B0, C0 = X0 + KD, X0 + KD + GROUPS
PROJ = 4 * KD + CONV_CH
MIXC = 2 * KD
PH = 8
NKEY = 128
TOPK = 16
RING = 4
N_IN, N_OUT, N_Q = PROJ, KD * MIXC // KD, 2 * PH
EPS = 1e-6
SCALE = HD ** -0.5
NEG = -1e30
HALF = NKEY // 2
GRP = 4
NG = NKEY // GRP
NGH = HALF // GRP

C_ID, C_ONE, C_SWAP, C_ROPC, C_ROPS, C_AM, C_CM, C_IOTA = np.cumsum([0, P, P, P, NT, NT, 3 * P, P]).tolist()
C_ALL = C_IOTA + P
(P_GMIX, P_CW, P_CB, P_DSK, P_GAT, P_GSSD, P_GFFN, P_GFIN, P_DTB, P_ALOG) = np.cumsum(
    [0, KD, CONV_CH * CONV_W, CONV_CH, KD, KD, KD, KD, KD, 1]).tolist()
P_ALL = P_ALOG + 1


def constants():
    c = np.zeros((P, C_ALL), np.float32)
    c[:, C_ID:C_ID + P] = np.eye(P)
    c[:, C_ONE:C_ONE + P] = 1.0
    half = ROT // 2
    inv = (np.float32(500000.0) ** (-np.arange(half, dtype=np.float32) / np.float32(half))).astype(np.float32)
    pos = np.concatenate([np.arange(TP), np.full(NB, PAST)]).astype(np.float32)
    ang = (pos[:, None] * inv[None, :]).astype(np.float32).T
    c[:, C_ROPC:C_ROPC + NT] = 1.0
    for h in (0, HD):
        for r in range(half):
            c[h + r, C_SWAP + h + half + r] = c[h + half + r, C_SWAP + h + r] = 1.0
            c[h + r, C_ROPC:C_ROPC + NT] = c[h + half + r, C_ROPC:C_ROPC + NT] = np.cos(ang[r])
            c[h + r, C_ROPS:C_ROPS + NT] = -np.sin(ang[r])
            c[h + half + r, C_ROPS:C_ROPS + NT] = np.sin(ang[r])
    i = np.arange(P)
    later = np.where(i[None, :] > i[:, None], np.float32(NEG), np.float32(0))
    c[:, C_AM:C_AM + P] = later
    c[:, C_AM + 2 * P:C_AM + 3 * P] = later
    c[:, C_CM:C_CM + P] = i[None, :] >= i[:, None]
    c[:, C_IOTA:C_IOTA + P] = i[None, :]
    sel = np.zeros((NH, KD, P), np.float32)
    for ch in range(KD):
        for p in range(P):
            sel[2 * ch + p // HD, ch, p] = 1.0
    return c, sel


def build(nc, t):
    ctx = ExitStack()
    with ctx:
        def sb(name, shape, dt=F32, where=ctx):
            return where.enter_context(nc.sbuf_tensor(name, shape, dt))

        def ps(name, where, shape=(P, 512)):
            return where.enter_context(nc.psum_tensor(name, list(shape), F32))

        stage_sems = []

        def sem(name):
            stage_sems.append(nc.alloc_semaphore(name=name))
            return stage_sems[-1]

        def lasting(name):
            return nc.alloc_semaphore(name=name)

        def recycle():
            nc.clear_and_free_semaphores(list(stage_sems))
            stage_sems.clear()
            nc.all_engine_barrier()

        cst = sb("cst", [P, C_ALL])
        par = sb("par", [P, P_ALL])
        ring = sb("ring", [P, RING, KD, P])
        res = sb("res", [P, KD, NT])
        xn = sb("xn", [P, KD, NT])
        rstd = sb("rstd", [P, 2, NT])
        ident = cst[:, C_ID:C_ID + P]
        ones = cst[:, C_ONE:C_ONE + P]
        swap = cst[:, C_SWAP:C_SWAP + P]
        rope_c = cst[:, C_ROPC:C_ROPC + NT]
        rope_s = cst[:, C_ROPS:C_ROPS + NT]
        amask = cst[:, C_AM:C_AM + 3 * P]
        cmask = cst[:, C_CM:C_CM + P]
        iota = cst[:, C_IOTA:C_IOTA + P]

        ring_full = [lasting(f"ring_full{s}") for s in range(RING)]
        ring_used = [lasting(f"ring_used{s}") for s in range(RING)]

        def chain(eng, name):
            s, n = sem(name), [0]

            def link(*ins):
                for x in ins:
                    x.then_inc(s, 1)
                n[0] += len(ins)
                eng.wait_ge(s, n[0])
            return link

        def chain_loop(eng, s, base):
            n = [0]

            def link(*ins):
                for x in ins:
                    x.then_inc(s, 1)
                n[0] += len(ins)
                eng.wait_ge(s, base + n[0])
            return link

        def opened(eng, *sems):
            for s in sems:
                eng.sem_inc(s, 1)

        def load_ring(sp, i):
            for s in range(RING):
                sp.wait_ge(ring_used[s], i + 1)
                sp.dma_start(ring[:, s], t["w_ring"][i * RING + s].rearrange("p (a b) -> p a b", a=KD)
                             ).then_inc(ring_full[s], 16)

        st = ctx.enter_context(ExitStack())
        mix = sb("mix", [P, MIXC, NT], where=st)
        proj = sb("proj", [P, PROJ, NT], where=st)
        wdt = sb("wdt", [P, KD, NH], where=st)
        dth = sb("dth", [NH, NT], where=st)
        with ExitStack() as s1:
            sq = sb("sq1", [P, KD, NT], where=s1)
            bank = [ps(f"pj{i}", s1) for i in range(RING)]
            sumb = ps("sum1", s1)
            dtb = ps("dt1", s1)
            loaded, squared, summed, root_in, rooted, normed = map(sem, (
                "in_loaded", "in_squared", "in_summed", "in_root_in", "in_rooted", "in_normed"))
            pj_copied = [sem(f"pj_copied{i}") for i in range(RING)]
            dt_ready, dt_copied = sem("dt_ready"), sem("dt_copied")
            with nc.Block() as block:
                @block.sync
                def _(sp):
                    with sp.Fori(0, N_IN // RING + 1) as i:
                        load_ring(sp, i)

                @block.scalar
                def _(act):
                    opened(act, pj_copied[0], pj_copied[2])
                    for dst, src in ((res[:], t["x"]), (cst[:], t["cst"]), (par[:], t["par"]), (wdt[:], t["w_dt"])):
                        act.dma_start(dst, src).then_inc(loaded, 16)
                    act.wait_ge(loaded, 64)
                    nc.scalar.activation(sq[:], res[:], ACT.Square).then_inc(squared, 1)
                    act.wait_ge(root_in, 1)
                    nc.scalar.activation(rstd[:, 0], rstd[:, 0], ACT.Sqrt).then_inc(rooted, 1)
                    with act.Fori(0, N_IN // RING) as i:
                        for s in (0, 2):
                            act.wait_ge(ring_used[s], i + 2)
                            nc.scalar.copy(proj[:, i * RING + s, :], bank[s][:, 0:NT]).then_inc(pj_copied[s], 1)
                    act.wait_ge(dt_ready, 1)
                    nc.scalar.copy(dth[:], dtb[0:NH, 0:NT]).then_inc(dt_copied, 1)
                    act.wait_ge(dt_copied, 1)

                @block.tensor
                def _(pe):
                    opened(pe, *ring_used)
                    pe.wait_ge(squared, 1)
                    for k in range(KD):
                        mm = nc.tensor.matmul(sumb[:, 0:NT], ones, sq[:, k], start=(k == 0), stop=(k == KD - 1))
                    mm.then_inc(summed, 1)
                    pe.wait_ge(normed, KD)
                    with pe.Fori(0, N_IN // RING) as i:
                        for s in range(RING):
                            pe.wait_ge(ring_full[s], 16 * i + 16)
                            pe.wait_ge(pj_copied[s], i + 1)
                            for k in range(KD):
                                mm = nc.tensor.matmul(bank[s][:, 0:NT], ring[:, s, k], xn[:, k],
                                                      start=(k == 0), stop=(k == KD - 1))
                            mm.then_inc(ring_used[s], 1)
                    for k in range(KD):
                        mm = nc.tensor.matmul(dtb[0:NH, 0:NT], wdt[:, k], xn[:, k], start=(k == 0), stop=(k == KD - 1))
                    mm.then_inc(dt_ready, 1)

                @block.vector
                def _(dve):
                    opened(dve, pj_copied[1], pj_copied[3])
                    link = chain(dve, "c_norm1")
                    dve.wait_ge(loaded, 64)
                    dve.wait_ge(summed, 1)
                    link(nc.vector.tensor_scalar(rstd[:, 1], sumb[:, 0:NT], 1.0 / D, EPS, ALU.mult, ALU.add))
                    nc.vector.reciprocal(rstd[:, 0], rstd[:, 1]).then_inc(root_in, 1)
                    dve.wait_ge(rooted, 1)
                    for k in range(KD):
                        nc.vector.scalar_tensor_tensor(out=xn[:, k], in0=res[:, k], scalar=par[:, P_GMIX + k:P_GMIX + k + 1],
                                                       in1=rstd[:, 0], op0=ALU.mult, op1=ALU.mult).then_inc(normed, 1)
                    with dve.Fori(0, N_IN // RING) as i:
                        for s in (1, 3):
                            dve.wait_ge(ring_used[s], i + 2)
                            nc.vector.tensor_copy(proj[:, i * RING + s, :], bank[s][:, 0:NT]).then_inc(pj_copied[s], 1)

        conv_s = sb("conv_s", [P, CONV_CH, NB, CONV_W], where=st)
        acs = sb("acs", [NH, TP], where=st)
        tokh = sb("tokh", [P, TT, 3, NH], where=st)
        dd = sb("dd", [NH, 2, NB], where=st)
        out_done = lasting("out_done")
        outs = [0]

        def store(eng, dst, src, n=1):
            outs[0] += n
            return eng.dma_start(dst, src).then_inc(out_done, 16)

        with ExitStack() as s2:
            cv = sb("cv", [P, CONV_CH, NT], where=s2)
            cs4 = sb("cs4", [P, CONV_CH, NB, CONV_W], where=s2)
            dtw = sb("dtw", [NH, 6, NT], where=s2)
            tps = ps("tps", s2)
            st_loaded, st_joined, acc_done, conv_done, silu_done = map(sem, (
                "conv_state", "conv_joined", "conv_acc", "conv_done", "silu_done"))
            raw_out = sem("raw_out")
            dt_a, dt_b, dt_c, dt_d, te_in, te_out, dec_in, acs_ready, tok_ready = map(sem, (
                "dt_abs", "dt_exp", "dt_one", "dt_log", "te_in", "te_out", "dec_in", "acs_ready", "tok_ready"))
            with nc.Block() as block:
                @block.sync
                def _(sp):
                    sp.dma_start(conv_s[:, :, :, 0:CONV_W - 1], t["state_conv"]).then_inc(st_loaded, 16)
                    sp.dma_start(t["conv_p"], proj[:, X0:X0 + CONV_CH, TP - 3:TP]).then_inc(raw_out, 16)
                    sp.wait_ge(raw_out, 16)

                @block.vector
                def _(dve):
                    link = chain(dve, "c_dt")
                    x, ab, e, u, w, q = (dtw[:, j] for j in range(6))
                    link(nc.vector.tensor_scalar(x, dth[:], par[0:NH, P_DTB:P_DTB + 1], None, ALU.add))
                    nc.vector.scalar_tensor_tensor(out=ab, in0=x, scalar=-1.0, in1=x, op0=ALU.mult, op1=ALU.max).then_inc(dt_a, 1)
                    dve.wait_ge(dt_b, 2)
                    nc.vector.tensor_scalar(u, e, 1.0, None, ALU.add).then_inc(dt_c, 1)
                    dve.wait_ge(dt_c, 1)
                    link(nc.vector.tensor_scalar(w, u, 1.0, None, ALU.subtract))
                    link(nc.vector.tensor_tensor(w, e, w, ALU.subtract), nc.vector.reciprocal(q, u))
                    link(nc.vector.tensor_tensor(w, w, q, ALU.mult))
                    dve.wait_ge(dt_d, 1)
                    link(nc.vector.tensor_tensor(w, w, ab, ALU.add))
                    link(nc.vector.scalar_tensor_tensor(out=dth[:], in0=x, scalar=0.0, in1=w, op0=ALU.max, op1=ALU.add))
                    link(nc.vector.tensor_scalar(u, dth[:], par[0:NH, P_ALOG:P_ALOG + 1], -1.0, ALU.mult, ALU.mult),
                         nc.vector.memset(q, 0.0))
                    for k in range(TT):
                        link(nc.vector.tensor_tensor_scan(acs[:, k * P:(k + 1) * P], u[:, k * P:(k + 1) * P],
                                                          q[:, k * P:(k + 1) * P], 0.0, ALU.add, ALU.add))
                    nc.vector.tensor_copy(dd[:, 0], u[:, TP:NT]).then_inc(dec_in, 1)
                    nc.vector.tensor_copy(dd[:, 1], dth[:, TP:NT]).then_inc(dec_in, 1)
                    for k in range(TT):
                        last = acs[:, (k + 1) * P - 1:(k + 1) * P]
                        nc.vector.tensor_scalar(x[:, k * P:(k + 1) * P], acs[:, k * P:(k + 1) * P], last, -1.0,
                                                ALU.subtract, ALU.mult).then_inc(te_in, 1)
                    dve.wait_ge(te_out, 2)
                    nc.vector.tensor_tensor(w[:, 0:TP], ab[:, 0:TP], dth[:, 0:TP], ALU.mult).then_inc(acs_ready, 1)
                    with dve.Fori(0, CONV_CH) as c:
                        cl = chain_loop(dve, acc_done, 4 * c)
                        cw = [par[:, bass.ds(c * CONV_W + (P_CW + j), 1)] for j in range(CONV_W)]
                        cl(nc.vector.tensor_scalar(cv[:, c, 0:TP], proj[:, c + X0, 0:TP], cw[3], None, ALU.mult))
                        for j in (1, 2, 3):
                            cl(nc.vector.scalar_tensor_tensor(out=cv[:, c, j:TP], in0=proj[:, c + X0, 0:TP - j],
                                                              scalar=cw[3 - j], in1=cv[:, c, j:TP], op0=ALU.mult, op1=ALU.add))
                    dve.wait_ge(st_loaded, 16)
                    nc.vector.tensor_copy(conv_s[:, :, :, 3], proj[:, X0:X0 + CONV_CH, TP:NT]).then_inc(st_joined, 1)
                    dve.wait_ge(st_joined, 1)
                    cwb = par[:, P_CW:P_CB].rearrange("p (c w) -> p c w", w=CONV_W).unsqueeze(2).broadcast_to(
                        [P, CONV_CH, NB, CONV_W])
                    link(nc.vector.tensor_tensor(cs4[:], conv_s[:], cwb, ALU.mult))
                    nc.vector.tensor_reduce(cv[:, :, TP:NT], cs4[:], AX_X, ALU.add).then_inc(conv_done, 1)
                    dve.wait_ge(tok_ready, 1)
                    nc.vector.tensor_copy(tokh[:].rearrange("p k j h -> p (k j h)"), tps[:, 0:TT * 3 * NH]).then_inc(acs_ready, 1)
                    dve.wait_ge(acs_ready, 2)

                @block.scalar
                def _(act):
                    act.wait_ge(dt_a, 1)
                    nc.scalar.activation(dtw[:, 2], dtw[:, 1], ACT.Exp, scale=-1.0).then_inc(dt_b, 1)
                    nc.scalar.activation(par[0:NH, P_ALOG:P_ALOG + 1], par[0:NH, P_ALOG:P_ALOG + 1], ACT.Exp).then_inc(dt_b, 1)
                    act.wait_ge(dt_c, 1)
                    nc.scalar.activation(dtw[:, 1], dtw[:, 3], ACT.Ln).then_inc(dt_d, 1)
                    act.wait_ge(dec_in, 2)
                    nc.scalar.activation(dd[:, 0], dd[:, 0], ACT.Exp).then_inc(te_out, 1)
                    act.wait_ge(te_in, TT)
                    nc.scalar.activation(dtw[:, 1, 0:TP], dtw[:, 0, 0:TP], ACT.Exp).then_inc(te_out, 1)
                    act.wait_ge(conv_done, 1)
                    act.wait_ge(raw_out, 16)
                    with act.Fori(0, CONV_CH) as c:
                        nc.scalar.activation(proj[:, c + X0, :], cv[:, c, :], ACT.Silu,
                                             bias=par[:, bass.ds(c + P_CB, 1)]).then_inc(silu_done, 1)
                    nc.scalar.activation(proj[:, Z0:Z0 + KD], proj[:, Z0:Z0 + KD], ACT.Silu).then_inc(silu_done, 1)
                    act.wait_ge(silu_done, CONV_CH + 1)

                @block.tensor
                def _(pe):
                    pe.wait_ge(acs_ready, 1)
                    for k in range(TT):
                        for j, src in enumerate((acs, dth, dtw[:, 4])):
                            at = (k * 3 + j) * NH
                            mm = nc.tensor.transpose(tps[:, at:at + NH], src[:, k * P:(k + 1) * P], cst[0:NH, C_ID:C_ID + NH])
                    mm.then_inc(tok_ready, 1)

        qkv_s = sb("qkv_s", [P, 3, KD, NB], where=st)
        with ExitStack() as s3:
            qk = sb("qk", [P, 2, NT], where=s3)
            tmp = sb("rtmp", [P, 2, NT], where=s3)
            vst = sb("vst", [P, TP], where=s3)
            vtok = sb("vtok", [P, TT, P], where=s3)
            sc = sb("scores", [P, 2, 3 * P], where=s3)
            pt = sb("probsT", [P, 2, 3 * P], where=s3)
            stat = sb("astat", [P, 2, 6], where=s3)
            sw, vb = ps("sw", s3), ps("vb", s3)
            sbk = [ps(f"s{j}", s3) for j in range(2)]
            ptb = [ps(f"pt{j}", s3) for j in range(2)]
            ob = [ps(f"o{j}", s3) for j in range(2)]
            (swapped, sw_free, rot, v_staged, v_turned, v_copied, qk_ready, k_out, s_ready, s_masked, maxed, expd, p_ready,
             p_turned, pt0_copied, pt1_copied, o_ready, o_copied, sam, summed3) = map(sem, (
                "swapped", "sw_free", "rot", "v_staged", "v_turned", "v_copied", "qk_ready", "k_out", "s_ready", "s_masked",
                "maxed", "expd", "p_ready", "p_turned", "pt0_copied", "pt1_copied", "o_ready", "o_copied", "sam", "rsum"))
            with nc.Block() as block:
                @block.sync
                def _(sp):
                    sp.dma_start(t["conv_s"], conv_s[:, :, :, 1:CONV_W]).then_inc(k_out, 16)
                    with sp.Fori(0, KD) as c:
                        sp.wait_ge(qk_ready, 2 * c + 2)
                        sp.dma_start(t["k_out"][:, c], qk[:, 1]).then_inc(k_out, 16)
                    sp.wait_ge(k_out, 16 * KD + 16)

                @block.tensor
                def _(pe):
                    opened(pe, s_ready, v_turned)
                    with pe.Fori(0, KD) as c:
                        for j, at in enumerate((Q0, K0)):
                            pe.wait_ge(sw_free, 2 * c + (j + 1))
                            nc.tensor.matmul(sw[:, 0:NT], swap, proj[:, c + at, :], start=True, stop=True).then_inc(swapped, 1)
                        pe.wait_ge(v_staged, c + 1)
                        pe.wait_ge(v_copied, c + 1)
                        for k in range(TT):
                            mm = nc.tensor.transpose(vb[:, k * P:(k + 1) * P], vst[:, k * P:(k + 1) * P], ident)
                        mm.then_inc(v_turned, 1)
                        pe.wait_ge(qk_ready, 2 * c + 2)
                        pe.wait_ge(o_copied, 2 * c + 1)
                        for j in range(2):
                            r = slice(j * HD, (j + 1) * HD)
                            nc.tensor.matmul(sbk[j][:, 0:P], qk[r, 0, 0:P], qk[r, 1, 0:P], start=True, stop=True)
                            nc.tensor.matmul(sbk[j][:, P:3 * P], qk[r, 0, P:TP], qk[r, 1, 0:TP],
                                             start=True, stop=True).then_inc(s_ready, 1)
                        for j in range(2):
                            pe.wait_ge(p_ready, 2 * c + j + 1)
                            nc.tensor.transpose(ptb[j][:, 0:P], sc[:, j, 0:P], ident)
                            nc.tensor.transpose(ptb[j][:, P:2 * P], sc[:, j, P:2 * P], ident)
                            nc.tensor.transpose(ptb[j][:, 2 * P:3 * P], sc[:, j, 2 * P:3 * P], ident).then_inc(p_turned, 1)
                        pe.wait_ge(v_copied, c + 2)
                        for j in range(2):
                            pe.wait_ge((pt0_copied, pt1_copied)[j], c + 1)
                            nc.tensor.matmul(ob[j][:, 0:P], vtok[:, 0], pt[:, j, 0:P], start=True, stop=True)
                            nc.tensor.matmul(ob[j][:, P:TP], vtok[:, 0], pt[:, j, P:2 * P], start=True, stop=False)
                            nc.tensor.matmul(ob[j][:, P:TP], vtok[:, 1], pt[:, j, 2 * P:3 * P], start=False,
                                             stop=True).then_inc(o_ready, 1)

                @block.vector
                def _(dve):
                    opened(dve, sw_free, v_copied)
                    with dve.Fori(0, KD) as c:
                        for j, at in enumerate((Q0, K0)):
                            if j == 1:
                                dve.wait_ge(k_out, 16 * c + 16)
                            else:
                                dve.wait_ge(s_ready, 2 * c + 1)
                            dve.wait_ge(swapped, 2 * c + j + 1)
                            nc.vector.tensor_tensor(tmp[:, 0], proj[:, c + at, :], rope_c, ALU.mult).then_inc(rot, 1)
                            nc.vector.tensor_tensor(tmp[:, 1], sw[:, 0:NT], rope_s, ALU.mult).then_inc(sw_free, 1)
                            dve.wait_ge(rot, 2 * c + j + 1)
                            dve.wait_ge(sw_free, 2 * c + (j + 2))
                            nc.vector.tensor_tensor(qk[:, j], tmp[:, 0], tmp[:, 1], ALU.add).then_inc(qk_ready, 1)
                            dve.wait_ge(qk_ready, 2 * c + j + 1)
                        dve.wait_ge(v_turned, c + 2)
                        nc.vector.tensor_copy(vtok[:].rearrange("p k f -> p (k f)"), vb[:, 0:TP]).then_inc(v_copied, 1)
                        sl = chain_loop(dve, s_masked, 6 * c)
                        for j in range(2):
                            dve.wait_ge(s_ready, 2 * c + (j + 2))
                            sl(nc.vector.tensor_tensor(sc[:, j], sbk[j][:, 0:3 * P], amask, ALU.add))
                            sl(nc.vector.tensor_reduce(stat[:, j, 0:1], sc[:, j, 0:P], AX_X, ALU.max),
                               nc.vector.tensor_reduce(stat[:, j, 1:2], sc[:, j, P:3 * P], AX_X, ALU.max))
                            nc.vector.tensor_scalar(stat[:, j, 0:2], stat[:, j, 0:2], -SCALE, None, ALU.mult).then_inc(maxed, 1)
                        for j in range(2):
                            dve.wait_ge(expd, 4 * c + 2 * j + 2)
                            nc.vector.reciprocal(stat[:, j, 4:6], stat[:, j, 2:4]).then_inc(summed3, 1)
                            dve.wait_ge(summed3, 2 * c + j + 1)
                            nc.vector.tensor_scalar(sc[:, j, 0:P], sc[:, j, 0:P], stat[:, j, 4:5], None, ALU.mult)
                            nc.vector.tensor_scalar(sc[:, j, P:3 * P], sc[:, j, P:3 * P], stat[:, j, 5:6], None,
                                                    ALU.mult).then_inc(p_ready, 1)
                        dve.wait_ge(p_turned, 2 * c + 2)
                        nc.vector.tensor_copy(pt[:, 1], ptb[1][:, 0:3 * P]).then_inc(pt1_copied, 1)

                @block.scalar
                def _(act):
                    opened(act, o_copied)
                    with act.Fori(0, KD) as c:
                        act.wait_ge(v_turned, c + 1)
                        nc.scalar.copy(vst[:], proj[:, c + V0, 0:TP]).then_inc(v_staged, 1)
                        nc.scalar.copy(qkv_s[:, 2, c, :], proj[:, c + V0, TP:NT]).then_inc(sam, 1)
                        act.wait_ge(qk_ready, 2 * c + 2)
                        nc.scalar.copy(qkv_s[:, 0:2, c, :], qk[:, :, TP:NT]).then_inc(sam, 1)
                        for j in range(2):
                            act.wait_ge(maxed, 2 * c + j + 1)
                            nc.scalar.activation(sc[:, j, 0:P], sc[:, j, 0:P], ACT.Exp, bias=stat[:, j, 0:1], scale=SCALE,
                                                 accum_out=stat[:, j, 2:3]).then_inc(expd, 1)
                            nc.scalar.activation(sc[:, j, P:3 * P], sc[:, j, P:3 * P], ACT.Exp, bias=stat[:, j, 1:2],
                                                 scale=SCALE, accum_out=stat[:, j, 3:4]).then_inc(expd, 1)
                        act.wait_ge(p_turned, 2 * c + 1)
                        nc.scalar.copy(pt[:, 0], ptb[0][:, 0:3 * P]).then_inc(pt0_copied, 1)
                        for j in range(2):
                            r = slice(j * HD, (j + 1) * HD)
                            act.wait_ge(o_ready, 2 * c + j + 1)
                            nc.scalar.copy(mix[r, c, 0:TP], ob[j][r, 0:TP]).then_inc(o_copied, 1)
                    act.wait_ge(o_copied, 2 * KD + 1)
                    act.wait_ge(sam, 2 * KD)

        with ExitStack() as s4:
            cb = sb("cb", [P, TT, GROUPS, P], where=s4)
            btok = sb("btok", [P, TT, GROUPS, P], where=s4)
            xst = sb("xst", [P, TP], where=s4)
            xtok = sb("xtok", [P, TT, P], where=s4)
            row = sb("row", [NH, 2, TP], where=s4)
            dec = sb("dec", [P, 2, TP], where=s4)
            wgt = sb("wgt", [P, 2, TP], where=s4)
            eb = sb("eb", [P, 2, P], where=s4)
            cs = sb("cs", [P, 2, P], where=s4)
            xw = sb("xw", [P, TT, P], where=s4)
            h0 = sb("h0", [P, P], where=s4)
            h1 = sb("h1", [P, P], where=s4)
            xb, hb0, hb1 = ps("xb", s4), ps("hb0", s4), ps("hb1", s4)
            bc = [ps(f"bc{j}", s4) for j in range(2)]
            yb = [ps(f"y{j}", s4) for j in range(2)]
            (cb_ready, cb_copied, x_staged, x_turned, x_copied, rows, bcd, d_ready, e_ready, eb_ready, w_ready, xw_ready,
             h0_ready, h0_copied, h1_ready, h1_done, h1_out, y_ready, y_done, cs_ready) = map(sem, (
                 "cb_ready", "cb_copied", "x_staged", "x_turned", "x_copied", "rows", "bcd", "d_ready", "e_ready", "eb_ready",
                 "w_ready", "xw_ready", "h0_ready", "h0_copied", "h1_ready", "h1_done", "h1_out", "y_ready", "y_done",
                 "cs_ready"))
            with nc.Block() as block:
                @block.sync
                def _(sp):
                    sp.dma_start(t["v_out"], proj[:, V0:V0 + KD]).then_inc(h1_out, 16)
                    with sp.Fori(0, KD) as c:
                        sp.wait_ge(h1_done, 2 * c + 3)
                        sp.dma_start(t["ssm_p"][:, c], h1[:]).then_inc(h1_out, 16)
                    sp.wait_ge(h1_out, 16 * KD + 16)

                @block.tensor
                def _(pe):
                    opened(pe, x_turned, y_ready, bcd, h1_ready)
                    for k in range(TT):
                        for g in range(GROUPS):
                            tk = slice(k * P, (k + 1) * P)
                            at = (k * GROUPS + g) * P
                            nc.tensor.matmul(bc[0][:, at:at + P], proj[:, B0 + g, tk], proj[:, C0 + g, tk], start=True, stop=True)
                            mm = nc.tensor.transpose(bc[1][:, at:at + P], proj[:, B0 + g, tk], ident)
                    mm.then_inc(cb_ready, 1)
                    pe.wait_ge(cb_copied, 2 * TT)
                    for g in range(GROUPS):
                        with pe.Fori(g * KD // GROUPS, (g + 1) * KD // GROUPS) as c:
                            pe.wait_ge(x_staged, c + 1)
                            for k in range(TT):
                                mm = nc.tensor.transpose(xb[:, k * P:(k + 1) * P], xst[:, k * P:(k + 1) * P], ident)
                            mm.then_inc(x_turned, 1)
                            for j in range(2):
                                pe.wait_ge(rows, 2 * c + j + 1)
                                nc.tensor.matmul(bc[j][:, 0:TP], cst[0:NH, C_ONE:C_ONE + P], row[:, j], start=True,
                                                 stop=True).then_inc(bcd, 1)
                            pe.wait_ge(xw_ready, 2 * c + 2)
                            pe.wait_ge(h0_copied, c + 1)
                            nc.tensor.matmul(hb0[:, 0:P], btok[:, 0, g], xw[:, 0], start=True, stop=True).then_inc(h0_ready, 1)
                            pe.wait_ge(h1_done, 2 * c + 1)
                            nc.tensor.matmul(hb1[:, 0:P], btok[:, 1, g], xw[:, 1], start=True, stop=True).then_inc(h1_ready, 1)
                            pe.wait_ge(h0_copied, c + 2)
                            pe.wait_ge(y_done, 2 * c + 1)
                            for j in range(2):
                                pe.wait_ge(w_ready, 4 * c + (2 * j + 3))
                                pe.wait_ge(cs_ready, 2 * c + j + 1)
                                nc.tensor.matmul(yb[j][:, 0:P], xtok[:, 0], wgt[:, j, 0:P], start=True, stop=True)
                                nc.tensor.matmul(yb[j][:, P:TP], xtok[:, 1], wgt[:, j, P:TP], start=True, stop=False)
                                nc.tensor.matmul(yb[j][:, P:TP], h0[:], cs[:, j], start=False, stop=True).then_inc(y_ready, 1)

                @block.scalar
                def _(act):
                    opened(act, h0_copied)
                    act.wait_ge(cb_ready, 1)
                    with act.Fori(0, KD) as c:
                        act.wait_ge(x_turned, c + 1)
                        nc.scalar.copy(xst[:], proj[:, c + X0, 0:TP]).then_inc(x_staged, 1)
                        for j in range(2):
                            act.wait_ge(bcd, 2 * c + (j + 2))
                            act.wait_ge(d_ready, 4 * c + 2 * j + 2)
                            act.wait_ge(h1_done, 2 * c + 1)
                            nc.scalar.activation(eb[:, j], bc[j][:, P:TP], ACT.Exp).then_inc(eb_ready, 1)
                            act.wait_ge(w_ready, 4 * c + 1)
                            nc.scalar.activation(dec[:, j], dec[:, j], ACT.Exp).then_inc(e_ready, 1)
                        act.wait_ge(h0_ready, c + 1)
                        act.wait_ge(y_ready, 2 * c + 1)
                        nc.scalar.copy(h0[:], hb0[:, 0:P]).then_inc(h0_copied, 1)

                @block.vector
                def _(dve):
                    opened(dve, h1_done, y_done, w_ready)
                    dve.wait_ge(cb_ready, 1)
                    for k in range(TT):
                        at = k * GROUPS * P
                        nc.vector.tensor_tensor(cb[:, k], bc[0][:, at:at + GROUPS * P].rearrange("p (g t) -> p g t", g=GROUPS),
                                                cmask.unsqueeze(1).broadcast_to([P, GROUPS, P]), ALU.mult).then_inc(cb_copied, 1)
                        nc.vector.tensor_copy(btok[:, k], bc[1][:, at:at + GROUPS * P].rearrange("p (g t) -> p g t", g=GROUPS)
                                              ).then_inc(cb_copied, 1)
                    dve.wait_ge(cb_copied, 2 * TT)
                    for g in range(GROUPS):
                        with dve.Fori(g * KD // GROUPS, (g + 1) * KD // GROUPS) as c:
                            for j in range(2):
                                dve.wait_ge(bcd, 2 * c + 1)
                                nc.vector.tensor_scalar(row[:, j], acs[:], cst[0:NH, bass.ds(c * 2 + j + C_ID, 1)], None,
                                                        ALU.mult).then_inc(rows, 1)
                            dve.wait_ge(x_turned, c + 2)
                            dve.wait_ge(y_ready, 2 * c + 1)
                            nc.vector.tensor_copy(xtok[:].rearrange("p k f -> p (k f)"), xb[:, 0:TP]).then_inc(x_copied, 1)
                            dve.wait_ge(x_copied, c + 1)
                            dve.wait_ge(h1_ready, c + 1)
                            for k in range(TT):
                                te = tokh[:, k, 2, bass.ds(c * 2, 2)].unsqueeze(2).broadcast_to([P, 2, HD])
                                nc.vector.tensor_tensor(xw[:, k].rearrange("p (j f) -> p j f", j=2),
                                                        xtok[:, k].rearrange("p (j f) -> p j f", j=2), te, ALU.mult
                                                        ).then_inc(xw_ready, 1)
                            for j in range(2):
                                dve.wait_ge(bcd, 2 * c + (j + 2))
                                for k in range(TT):
                                    nc.vector.tensor_scalar(dec[:, j, k * P:(k + 1) * P], bc[j][:, k * P:(k + 1) * P],
                                                            tokh[:, k, 0, bass.ds(c * 2 + j, 1)], 0.0, ALU.subtract, ALU.min
                                                            ).then_inc(d_ready, 1)
                            for j in range(2):
                                dve.wait_ge(e_ready, 2 * c + j + 1)
                                for k in range(TT):
                                    nc.vector.scalar_tensor_tensor(out=wgt[:, j, k * P:(k + 1) * P], in0=dec[:, j, k * P:(k + 1) * P],
                                                                   scalar=tokh[:, k, 1, bass.ds(c * 2 + j, 1)], in1=cb[:, k, g],
                                                                   op0=ALU.mult, op1=ALU.mult).then_inc(w_ready, 1)
                                dve.wait_ge(eb_ready, 2 * c + j + 1)
                                nc.vector.tensor_tensor(cs[:, j], eb[:, j], proj[:, C0 + g, P:TP], ALU.mult).then_inc(cs_ready, 1)
                            dve.wait_ge(h1_ready, c + 2)
                            dve.wait_ge(h0_copied, c + 2)
                            dve.wait_ge(h1_out, 16 * c + 16)
                            for j in range(2):
                                f = slice(j * HD, (j + 1) * HD)
                                nc.vector.scalar_tensor_tensor(out=h1[:, f], in0=h0[:, f], scalar=eb[:, j, P - 1:P], in1=hb1[:, f],
                                                               op0=ALU.mult, op1=ALU.add).then_inc(h1_done, 1)
                            for j in range(2):
                                r = slice(j * HD, (j + 1) * HD)
                                dve.wait_ge(y_ready, 2 * c + (j + 2))
                                nc.vector.scalar_tensor_tensor(out=mix[r, c + KD, 0:TP], in0=proj[r, c + X0, 0:TP],
                                                               scalar=par[r, bass.ds(c + P_DSK, 1)], in1=yb[j][r, 0:TP],
                                                               op0=ALU.mult, op1=ALU.add).then_inc(y_done, 1)
                    dve.wait_ge(y_done, 2 * KD + 1)

        recycle()
        with ExitStack() as s5:
            sel = sb("sel", [NH, KD, P], where=s5)
            hs = sb("hs", [P, KD, NB, P], where=s5)
            bcb = sb("bcb", [P, 2, GROUPS, NB, P], where=s5)
            ex = sb("ex", [P, 2, GROUPS, NB, P], where=s5)
            dds = sb("dds", [P, KD, 2, NB], where=s5)
            xdt = sb("xdt", [P, KD, NB], where=s5)
            u5 = sb("u5", [P, NB, P], where=s5)
            pb = [ps(f"b5_{i}", s5) for i in range(2 * GROUPS * NB * P // 512)]
            (h_loaded, ex_done, bc_done, bc_out, dd_done, xdt_done, c5, y5, hs_out, sel_loaded, hdec) = map(sem, (
                "h_loaded", "ex_done", "bc_done", "bc_out", "dd_done", "xdt_done", "c5", "y5", "hs_out", "sel_loaded", "hdec"))
            with nc.Block() as block:
                @block.sync
                def _(sp):
                    sp.dma_start(sel[:], t["sel"]).then_inc(sel_loaded, 16)
                    sp.dma_start(hs[:], t["state_ssm"]).then_inc(h_loaded, 16)
                    with sp.Fori(0, KD) as c:
                        sp.wait_ge(y5, c + 1)
                        sp.dma_start(t["ssm_s"][:, c], hs[:, c]).then_inc(hs_out, 16)
                    sp.wait_ge(hs_out, 16 * KD)

                @block.tensor
                def _(pe):
                    pe.wait_ge(sel_loaded, 16)
                    for c in range(KD):
                        mm = nc.tensor.matmul(pb[0][:, c * 2 * NB:(c + 1) * 2 * NB], sel[:, c], dd[:].rearrange("h a b -> h (a b)"),
                                              start=True, stop=True)
                    mm.then_inc(dd_done, 1)
                    pe.wait_ge(xdt_done, 1)
                    pe.wait_ge(ex_done, 2)
                    flat = ex[:].rearrange("p a g b n -> p (a g b n)")
                    for i, b in enumerate(pb):
                        nc.tensor.matmul(b[:], ones, flat[:, i * 512:(i + 1) * 512], start=True, stop=True).then_inc(bc_done, 1)

                @block.scalar
                def _(act):
                    flat = bcb[:].rearrange("p a g b n -> p (a g b n)")
                    for i, b in enumerate(pb):
                        act.wait_ge(bc_done, i + 1)
                        nc.scalar.copy(flat[:, i * 512:(i + 1) * 512], b[:]).then_inc(bc_out, 1)

                @block.gpsimd
                def _(pool):
                    pool.wait_ge(h_loaded, 16)
                    pool.wait_ge(xdt_done, 1)
                    with pool.Fori(0, KD) as c:
                        nc.gpsimd.tensor_tensor(hs[:, c], hs[:, c], dds[:, c, 0, :].unsqueeze(2).broadcast_to([P, NB, P]),
                                                ALU.mult).then_inc(hdec, 1)

                @block.vector
                def _(dve):
                    dve.wait_ge(dd_done, 1)
                    link = chain(dve, "c_five")
                    link(nc.vector.tensor_copy(dds[:].rearrange("p c a b -> p (c a b)"), pb[0][:, 0:KD * 2 * NB]))
                    nc.vector.tensor_tensor(xdt[:], proj[:, X0:X0 + KD, TP:NT], dds[:, :, 1], ALU.mult).then_inc(xdt_done, 1)
                    for a, at in enumerate((B0, C0)):
                        nc.vector.tensor_tensor(ex[:, a], ident.unsqueeze(1).unsqueeze(1).broadcast_to([P, GROUPS, NB, P]),
                                                proj[:, at:at + GROUPS, TP:NT].unsqueeze(3).broadcast_to([P, GROUPS, NB, P]),
                                                ALU.mult).then_inc(ex_done, 1)
                    dve.wait_ge(xdt_done, 1)
                    dve.wait_ge(bc_out, len(pb))
                    for g in range(GROUPS):
                        with dve.Fori(g * KD // GROUPS, (g + 1) * KD // GROUPS) as c:
                            cl = chain_loop(dve, c5, 4 * c)
                            cl(nc.vector.tensor_tensor(u5[:], bcb[:, 0, g], xdt[:, c].unsqueeze(2).broadcast_to([P, NB, P]),
                                                       ALU.mult))
                            dve.wait_ge(hdec, c + 1)
                            nc.vector.tensor_tensor(hs[:, c], hs[:, c], u5[:], ALU.add).then_inc(y5, 1)
                            dve.wait_ge(y5, c + 1)
                            cl(nc.vector.tensor_tensor(u5[:], hs[:, c], bcb[:, 1, g], ALU.mult))
                            cl(nc.vector.tensor_reduce(mix[:, c + KD, TP:NT], u5[:], AX_X, ALU.add))
                            cl(nc.vector.scalar_tensor_tensor(out=mix[:, c + KD, TP:NT], in0=proj[:, c + X0, TP:NT],
                                                              scalar=par[:, bass.ds(c + P_DSK, 1)], in1=mix[:, c + KD, TP:NT],
                                                              op0=ALU.mult, op1=ALU.add))


        with ExitStack() as s6:
            ptab = sb("ptab", [1, NB * NPG], I32, where=s6)
            kt = sb("kt", [P, 2, NPG, KD, PAGE], where=s6)
            vt = sb("vt", [P, 2, NPG, D], where=s6)
            qbd = sb("qbd", [P, NB, KD, 2], where=s6)
            pr = sb("pr", [P, NB, KD, 2], where=s6)
            st6 = sb("st6", [P, NPG * P], where=s6)
            p6 = sb("p6", [P, PAST + 1], where=s6)
            pts = sb("pts", [P, NPG + 1, P], where=s6)
            dg = sb("dg", [P, P], where=s6)
            a6 = sb("a6", [P, 4], where=s6)
            o6 = sb("o6", [P, KD, NB], where=s6)
            stb, ssb, ptb6, ob6 = (ps(n, s6) for n in ("stb", "ssb", "ptb6", "ob6"))
            (pt_loaded, zeroed, q_spread, st_copied, ss_ready, max6, exp6, sum6, p6_ready, dg_ready, pt6_ready,
             pts_ready, c6) = map(sem, (
                 "pt_loaded", "zeroed", "q_spread", "st_copied", "ss_ready", "max6", "exp6", "sum6", "p6_ready",
                 "dg_ready", "pt6_ready", "pts_ready", "c6"))
            k_full = [sem(f"k_full{s}") for s in range(2)]
            v_full = [sem(f"v_full{s}") for s in range(2)]
            k_used = [sem(f"k_used{s}") for s in range(2)]
            v_used = [sem(f"v_used{s}") for s in range(2)]
            with nc.Block() as block:
                @block.sync
                def _(sp):
                    sp.dma_start(ptab[:], t["page_table"]).then_inc(pt_loaded, 16)
                    sp.wait_ge(pt_loaded, 16)
                    for what, full, used in (("k", k_full, k_used), ("v", v_full, v_used)):
                        with sp.Fori(0, NB // 2) as i:
                            for s in range(2):
                                sp.wait_ge(used[s], i + 1)
                                for g in range(NPG):
                                    page = sp.value_load(ptab[0:1, bass.ds(i * (2 * NPG) + (s * NPG + g), 1)], min_val=0,
                                                         max_val=t["n_pool"] - 1)
                                    if what == "k":
                                        sp.dma_start(kt[:, s, g].rearrange("p c n -> p (c n)"),
                                                     t["cache_k"][bass.ds(page, 1)].rearrange("a p n -> p (a n)")
                                                     ).then_inc(full[s], 16)
                                    else:
                                        sp.dma_start(vt[:, s, g], t["cache_v"][bass.ds(page, 1)].rearrange("a p n -> p (a n)")
                                                     ).then_inc(full[s], 16)

                @block.tensor
                def _(pe):
                    opened(pe, *k_used, *v_used)
                    pe.wait_ge(q_spread, 4)
                    with pe.Fori(0, NB // 2) as i:
                        for s in range(2):
                            pe.wait_ge(k_full[s], 16 * NPG * i + 16 * NPG)
                            for g in range(NPG):
                                for c in range(KD):
                                    mm = nc.tensor.matmul(stb[:, bass.ds(i * (2 * NH) + (g * P + s * NH + 2 * c), 2)], kt[:, s, g, c],
                                                          qbd[:, i * 2 + s, c, :], start=True, stop=True)
                            mm.then_inc(k_used[s], 1)
                    pe.wait_ge(st_copied, 1)
                    for g in range(NPG):
                        nc.tensor.transpose(ssb[:, g * P:(g + 1) * P], st6[:, g * P:(g + 1) * P], ident)
                    nc.tensor.matmul(ssb[:, PAST:PAST + 1], pr[:].rearrange("p b c j -> p (b c j)"), ones[:, 0:1],
                                     start=True, stop=True).then_inc(ss_ready, 1)
                    pe.wait_ge(p6_ready, 1)
                    for g in range(NPG):
                        nc.tensor.transpose(ptb6[:, g * P:(g + 1) * P], p6[:, g * P:(g + 1) * P], ident)
                    pe.wait_ge(dg_ready, 1)
                    nc.tensor.matmul(ptb6[:, PAST:PAST + P], ones, dg[:], start=True, stop=True).then_inc(pt6_ready, 1)
                    pe.wait_ge(pts_ready, 1)
                    with pe.Fori(0, NB // 2) as i:
                        for s in range(2):
                            pe.wait_ge(v_full[s], 16 * NPG * i + 16 * NPG)
                            for c in range(KD):
                                for g in range(NPG):
                                    mm = nc.tensor.matmul(ob6[:, bass.ds(i * (2 * NH) + (s * NH + 2 * c), 2)],
                                                          vt[:, s, g, c * P:(c + 1) * P],
                                                          pts[:, g, bass.ds(i * (2 * NH) + (s * NH + 2 * c), 2)],
                                                          start=(g == 0), stop=(g == NPG - 1))
                            mm.then_inc(v_used[s], 1)

                @block.scalar
                def _(act):
                    act.wait_ge(max6, 1)
                    nc.scalar.activation(p6[:], ssb[:, 0:PAST + 1], ACT.Exp, bias=a6[:, 1:2], scale=SCALE,
                                         accum_out=a6[:, 2:3]).then_inc(exp6, 1)

                @block.vector
                def _(dve):
                    nc.vector.memset(qbd[:], 0.0).then_inc(zeroed, 1)
                    nc.vector.memset(pr[:], 0.0).then_inc(zeroed, 1)
                    dve.wait_ge(zeroed, 2)
                    for j in range(2):
                        r = slice(j * HD, (j + 1) * HD)
                        q, k = (qkv_s[r, n].rearrange("p c b -> p b c") for n in range(2))
                        nc.vector.tensor_copy(qbd[r, :, :, j], q).then_inc(q_spread, 1)
                        nc.vector.tensor_tensor(pr[r, :, :, j], q, k, ALU.mult).then_inc(q_spread, 1)
                    for s in range(2):
                        dve.wait_ge(k_used[s], NB // 2 + 1)
                    nc.vector.tensor_copy(st6[:], stb[:, 0:NPG * P]).then_inc(st_copied, 1)
                    dve.wait_ge(ss_ready, 1)
                    nc.vector.tensor_reduce(a6[:, 0:1], ssb[:, 0:PAST + 1], AX_X, ALU.max).then_inc(c6, 1)
                    dve.wait_ge(c6, 1)
                    nc.vector.tensor_scalar(a6[:, 1:2], a6[:, 0:1], -SCALE, None, ALU.mult).then_inc(max6, 1)
                    dve.wait_ge(exp6, 1)
                    nc.vector.reciprocal(a6[:, 3:4], a6[:, 2:3]).then_inc(sum6, 1)
                    dve.wait_ge(sum6, 1)
                    nc.vector.tensor_scalar(p6[:], p6[:], a6[:, 3:4], None, ALU.mult).then_inc(p6_ready, 1)
                    dve.wait_ge(p6_ready, 1)
                    nc.vector.tensor_scalar(dg[:], ident, p6[:, PAST:PAST + 1], None, ALU.mult).then_inc(dg_ready, 1)
                    dve.wait_ge(pt6_ready, 1)
                    nc.vector.tensor_copy(pts[:].rearrange("p g n -> p (g n)"), ptb6[:, 0:PAST + P]).then_inc(pts_ready, 1)
                    dve.wait_ge(pts_ready, 1)
                    for j in range(2):
                        r = slice(j * HD, (j + 1) * HD)
                        own = pts[r, NPG].rearrange("p (b c j) -> p j c b", b=NB, j=2)[:, j]
                        nc.vector.tensor_tensor(o6[r], qkv_s[r, 2], own, ALU.mult).then_inc(c6, 1)
                    dve.wait_ge(c6, 3)
                    for s in range(2):
                        dve.wait_ge(v_used[s], NB // 2 + 1)
                    for j in range(2):
                        r = slice(j * HD, (j + 1) * HD)
                        past = ob6[r, 0:P].rearrange("p (b c j) -> p j c b", b=NB, j=2)[:, j]
                        nc.vector.tensor_tensor(mix[r, 0:KD, TP:NT], past, o6[r], ALU.add).then_inc(c6, 1)
                    dve.wait_ge(c6, 5)

        with ExitStack() as s7:
            sq = sb("sq7", [P, MIXC, NT], where=s7)
            rr = sb("rr7", [P, 4, NT], where=s7)
            nb7 = [ps(f"n7_{i}", s7) for i in range(4)]
            ob7 = [ps(f"o7_{i}", s7) for i in range(2)]
            (gated, sq7, sum7, var7, root7, mixed, res_done, sq8, sum8, var8, root8, xn_done) = map(sem, (
                "gated", "sq7", "sum7", "var7", "root7", "mixed", "res_done", "sq8", "sum8", "var8", "root8",
                "xn_done"))
            with nc.Block() as block:
                @block.sync
                def _(sp):
                    with sp.Fori(N_IN // RING + 1, (N_IN + N_OUT) // RING + 1) as i:
                        load_ring(sp, i)

                @block.scalar
                def _(act):
                    nc.scalar.activation(sq[:, 0:KD], mix[:, 0:KD], ACT.Square).then_inc(sq7, 1)
                    act.wait_ge(gated, 1)
                    nc.scalar.activation(sq[:, KD:MIXC], mix[:, KD:MIXC], ACT.Square).then_inc(sq7, 1)
                    act.wait_ge(var7, 1)
                    nc.scalar.activation(rr[:, 0:3], rr[:, 0:3], ACT.Sqrt).then_inc(root7, 1)
                    act.wait_ge(res_done, KD + 1)
                    nc.scalar.activation(sq[:, 0:KD], res[:], ACT.Square).then_inc(sq8, 1)
                    act.wait_ge(var8, 1)
                    nc.scalar.activation(rr[:, 3], rr[:, 3], ACT.Sqrt).then_inc(root8, 1)

                @block.tensor
                def _(pe):
                    pe.wait_ge(sq7, 2)
                    for n, (a, b) in enumerate(((0, 8), (8, 12), (12, 16))):
                        for k in range(a, b):
                            mm = nc.tensor.matmul(nb7[n][:, 0:NT], ones, sq[:, k], start=(k == a), stop=(k == b - 1))
                    mm.then_inc(sum7, 1)
                    pe.wait_ge(mixed, MIXC)
                    with pe.Fori(0, N_OUT // RING) as i:
                        for m in range(2):
                            pe.wait_ge(res_done, i * 2 + 1)
                            for a in range(2):
                                s = 2 * m + a
                                pe.wait_ge(ring_full[s], 16 * i + 16 * (N_IN // RING + 1))
                                for k in range(KD):
                                    mm = nc.tensor.matmul(ob7[m][:, 0:NT], ring[:, s, k], mix[:, a * KD + k],
                                                          start=(a == 0 and k == 0), stop=(a == 1 and k == KD - 1))
                                mm.then_inc(ring_used[s], 1)
                    pe.wait_ge(sq8, 1)
                    for k in range(KD):
                        mm = nc.tensor.matmul(nb7[3][:, 0:NT], ones, sq[:, k], start=(k == 0), stop=(k == KD - 1))
                    mm.then_inc(sum8, 1)

                @block.vector
                def _(dve):
                    opened(dve, res_done)
                    link = chain(dve, "c_seven")
                    nc.vector.tensor_tensor(mix[:, KD:MIXC], mix[:, KD:MIXC], proj[:, Z0:Z0 + KD], ALU.mult).then_inc(gated, 1)
                    dve.wait_ge(sum7, 1)
                    link(*[nc.vector.tensor_scalar(rr[:, n], nb7[n][:, 0:NT], 1.0 / w, EPS, ALU.mult, ALU.add)
                           for n, w in enumerate((D, D // GROUPS, D // GROUPS))])
                    nc.vector.reciprocal(rr[:, 0:3], rr[:, 0:3]).then_inc(var7, 1)
                    dve.wait_ge(root7, 1)
                    for k in range(MIXC):
                        n = 0 if k < KD else 1 + (k - KD) // (KD // GROUPS)
                        nc.vector.scalar_tensor_tensor(out=mix[:, k], in0=mix[:, k], scalar=par[:, P_GAT + k:P_GAT + k + 1],
                                                       in1=rr[:, n], op0=ALU.mult, op1=ALU.mult).then_inc(mixed, 1)
                    with dve.Fori(0, KD // 2) as i:
                        for m in range(2):
                            dve.wait_ge(ring_used[2 * m + 1], i + (N_IN // RING + 2))
                            nc.vector.tensor_tensor(res[:, i * 2 + m, :], res[:, i * 2 + m, :], ob7[m][:, 0:NT],
                                                    ALU.add).then_inc(res_done, 1)
                    dve.wait_ge(sum8, 1)
                    link(nc.vector.tensor_scalar(rr[:, 3], nb7[3][:, 0:NT], 1.0 / D, EPS, ALU.mult, ALU.add))
                    nc.vector.reciprocal(rr[:, 3], rr[:, 3]).then_inc(var8, 1)
                    dve.wait_ge(root8, 1)
                    for k in range(KD):
                        nc.vector.scalar_tensor_tensor(out=xn[:, k], in0=res[:, k], scalar=par[:, P_GFFN + k:P_GFFN + k + 1],
                                                       in1=rr[:, 3], op0=ALU.mult, op1=ALU.mult).then_inc(xn_done, 1)
                    dve.wait_ge(xn_done, KD)
        st.close()

        recycle()
        ig = sb("ig", [P, 3, NT])
        HK = PH * TOPK
        with ExitStack() as s8:
            keys = sb("keys", [P, 2 * PH, NKEY], where=s8)
            qst = sb("qst", [P, RING, NT], where=s8)
            stg = sb("stg", [P, RING, TILES, NKEY], where=s8)
            rest = sb("rest", [P, TILES, NKEY], where=s8)
            sv = sb("sv", [P, TILES, 2, TOPK], where=s8)
            si = sb("si", [P, TILES, 2, TOPK], U32, where=s8)
            cand = sb("cand", [P, TILES, 2, TOPK * TOPK], where=s8)
            best = sb("best", [P, TILES, TOPK], where=s8)
            bi = sb("bi", [P, TILES, TOPK], U32, where=s8)
            sif = sb("sif", [P, TILES, 2, PH, TOPK], where=s8)
            bests = sb("bests", [P, TILES, PH, TOPK], where=s8)
            bis = sb("bis", [P, TILES, PH, TOPK], U32, where=s8)
            ab = sb("ab", [P, 2, TILES, HK], U32, where=s8)
            abf = sb("abf", [P, 2, TILES, HK], where=s8)
            gs = sb("gs", [P, TILES, PH, TOPK], where=s8)
            tick = sb("tick", [P, 2], where=s8)
            rs = sb("rs8", [P, TILES, PH], where=s8)
            eq = sb("eq", [P, HK, TOPK], where=s8)
            found = sb("found", [P, 2, TILES, HK], where=s8)
            qb = [ps(f"q8_{i}", s8) for i in range(RING)]
            scb = [ps(f"sc8_{i}", s8) for i in range(2)]
            tb = [ps(f"t8_{i}", s8) for i in range(2)]
            keys_in, cleared, best_done, fin8, exp8, found_done, turned8, ig_done = map(sem, (
                "keys_in", "cleared", "best_done", "fin8", "exp8", "found_done", "turned8", "ig_done"))
            q_copied = [sem(f"q_copied{i}") for i in range(RING)]
            sc_ready = [sem(f"sc_ready{i}") for i in range(2)]
            sc_copied = [sem(f"sc_copied{i}") for i in range(2)]
            head_done = [sem(f"head_done{i}") for i in range(2)]
            base = (N_IN + N_OUT) // RING
            order = [("q", 0), ("q", 1), ("s", 0), ("q", 2), ("s", 1), ("q", 3), ("s", 2), ("s", 3)]
            with nc.Block() as block:
                @block.sync
                def _(sp):
                    sp.dma_start(keys[:], t["keys"]).then_inc(keys_in, 16)
                    with sp.Fori(base + 1, base + N_Q // RING) as i:
                        load_ring(sp, i)

                @block.tensor
                def _(pe):
                    opened(pe, *sc_ready)
                    pe.wait_ge(keys_in, 16)
                    pe.wait_ge(cleared, 5)
                    with pe.Fori(0, N_Q // RING) as i:
                        for kind, s in order:
                            if kind == "q":
                                pe.wait_ge(ring_full[s], 16 * i + 16 * (base + 1))
                                pe.wait_ge(q_copied[s], i + 1)
                                for k in range(KD):
                                    mm = nc.tensor.matmul(qb[s][:, 0:NT], ring[:, s, k], xn[:, k], start=(k == 0), stop=(k == KD - 1))
                                mm.then_inc(ring_used[s], 1)
                            else:
                                b = s % 2
                                pe.wait_ge(q_copied[s], i + 2)
                                pe.wait_ge(sc_copied[b], i * 4 + (2 * (s // 2) + 1))
                                for k in range(TILES):
                                    n = min(P, NT - k * P)
                                    mm = nc.tensor.matmul(scb[b][0:n, k * P:(k + 1) * P], qst[:, s, k * P:k * P + n],
                                                          keys[:, i * RING + s, :], start=True, stop=True)
                                mm.then_inc(sc_ready[b], 1)
                    pe.wait_ge(found_done, 2 * TILES)
                    pe.wait_ge(fin8, 2)
                    for n, src in enumerate((found[:, 0], found[:, 1], gs[:].rearrange("p t h k -> p t (h k)"))):
                        for k in range(TILES):
                            w = min(P, NT - k * P)
                            if n == 2 and k == 0:
                                pe.wait_ge(ig_done, 1)
                            mm = nc.tensor.transpose(tb[n % 2][:, k * P:k * P + w], src[0:w, k, :], cst[0:w, C_ID:C_ID + w])
                        mm.then_inc(turned8, 1)

                @block.scalar
                def _(act):
                    opened(act, *q_copied, *sc_copied)
                    with act.Fori(0, N_Q // RING) as i:
                        for kind, s in order:
                            b = s % 2
                            if kind == "q":
                                act.wait_ge(ring_used[s], i + (base + 2))
                                act.wait_ge(sc_ready[b], i * 2 + 1)
                                nc.scalar.copy(qst[:, s], qb[s][:, 0:NT]).then_inc(q_copied[s], 1)
                            else:
                                act.wait_ge(sc_ready[b], i * 2 + (s // 2 + 2))
                                act.wait_ge(head_done[s // 2], i + 1)
                                nc.scalar.copy(stg[:, s, 0:TT].rearrange("p t n -> p (t n)"), scb[b][:, 0:TP]).then_inc(sc_copied[b], 1)
                                nc.scalar.copy(stg[0:NB, s, TT], scb[b][0:NB, TP:TP + P]).then_inc(sc_copied[b], 1)
                    act.wait_ge(fin8, 1)
                    nc.scalar.activation(gs[:], gs[:], ACT.Exp).then_inc(exp8, 1)

                @block.vector
                def _(dve):
                    opened(dve, *head_done)
                    for x in (sv, si, best, bi, stg):
                        nc.vector.memset(x[:], 0).then_inc(cleared, 1)
                    dve.wait_ge(cleared, 5)
                    rows = [slice(0, min(P, NT - k * P)) for k in range(TILES)]
                    steps = sem("topk_steps")
                    with dve.Fori(0, N_Q // RING) as i:
                        for hh in range(2):
                            for b in range(2):
                                dve.wait_ge(sc_copied[b], i * 4 + (2 * hh + 3))
                            nc.vector.memset(tick[:, 0:1], 0.0)
                            dve.sem_clear(steps)
                            link = chain_loop(dve, steps, 0)

                            def top16(src, spare, val, idx):
                                link(*[nc.vector.max(val(k)[:, 0:8], src(k)) for k in range(TILES)])
                                link(*[nc.vector.max_index(idx(k)[:, 0:8], val(k)[:, 0:8], src(k)) for k in range(TILES)])
                                link(*[nc.vector.match_replace(spare(k), val(k)[:, 0:8], src(k), -3e38) for k in range(TILES)])
                                link(*[nc.vector.max(val(k)[:, 8:16], spare(k)) for k in range(TILES)])
                                link(*[nc.vector.max_index(idx(k)[:, 8:16], val(k)[:, 8:16], spare(k)) for k in range(TILES)])

                            for side in range(2):
                                top16(lambda k: stg[rows[k], 2 * hh + side, k], lambda k: rest[rows[k], k],
                                      lambda k: sv[rows[k], k, side], lambda k: si[rows[k], k, side])
                            link(*[nc.vector.tensor_tensor(
                                cand[rows[k], k, 0].rearrange("p (a b) -> p a b", a=TOPK),
                                sv[rows[k], k, 0].unsqueeze(2).broadcast_to([rows[k].stop, TOPK, TOPK]),
                                sv[rows[k], k, 1].unsqueeze(1).broadcast_to([rows[k].stop, TOPK, TOPK]), ALU.add)
                                for k in range(TILES)])
                            top16(lambda k: cand[rows[k], k, 0], lambda k: cand[rows[k], k, 1],
                                  lambda k: best[rows[k], k], lambda k: bi[rows[k], k])
                            nc.vector.tensor_copy(sif[:, :, :, i * 2 + hh, :], si[:]).then_inc(best_done, 1)
                            nc.vector.tensor_copy(bests[:, :, i * 2 + hh, :], best[:]).then_inc(best_done, 1)
                            nc.vector.tensor_copy(bis[:, :, i * 2 + hh, :], bi[:]).then_inc(best_done, 1)
                            dve.wait_ge(best_done, i * 6 + 3 * (hh + 1))
                            nc.vector.tensor_copy(tick[:, 1:2], best[:, 0, 0:1]).then_inc(head_done[hh], 1)
                            dve.wait_ge(head_done[hh], i + 2)
                    nc.vector.tensor_tensor(gs[:], bests[:], bests[:, :, :, 0:1].broadcast_to([P, TILES, PH, TOPK]),
                                            ALU.subtract).then_inc(fin8, 1)
                    link = chain(dve, "c_eight")
                    fl = bis[:].rearrange("p t h k -> p t (h k)")
                    link(nc.vector.tensor_single_scalar(ab[:, 0], fl, 4, ALU.logical_shift_right),
                         nc.vector.tensor_single_scalar(ab[:, 1], fl, 15, ALU.bitwise_and))
                    link(nc.vector.tensor_copy(abf[:], ab[:]))
                    for side in range(2):
                        for k in range(TILES):
                            link(nc.vector.tensor_tensor(eq[:], abf[:, side, k].unsqueeze(2).broadcast_to([P, HK, TOPK]),
                                                         iota[:, 0:TOPK].unsqueeze(1).broadcast_to([P, HK, TOPK]), ALU.is_equal))
                            e4 = eq[:].rearrange("p (h k) a -> p h k a", h=PH)
                            link(nc.vector.tensor_tensor(e4, e4, sif[:, k, side].unsqueeze(2).broadcast_to([P, PH, TOPK, TOPK]),
                                                         ALU.mult))
                            nc.vector.tensor_reduce(found[:, side, k], eq[:], AX_X, ALU.add).then_inc(found_done, 1)
                            dve.wait_ge(found_done, side * TILES + k + 1)
                    dve.wait_ge(exp8, 1)
                    link(nc.vector.tensor_reduce(rs[:], gs[:], AX_X, ALU.add))
                    link(nc.vector.reciprocal(rs[:], rs[:]))
                    nc.vector.tensor_tensor(gs[:], gs[:], rs[:].unsqueeze(3).broadcast_to([P, TILES, PH, TOPK]),
                                            ALU.mult).then_inc(fin8, 1)
                    for n in range(3):
                        dve.wait_ge(turned8, n + 1)
                        nc.vector.tensor_copy(ig[:, n], tb[n % 2][:, 0:NT]).then_inc(ig_done, 1)
                    dve.wait_ge(ig_done, 3)

        with ExitStack() as s9:
            gw = sb("gw", [P, NT, HALF], where=s9)
            av = sb("av", [P, 2, 8, P], where=s9)
            bv = sb("bv", [P, 2, 8, HALF], where=s9)
            ub = sb("ub", [P, GRP, KD, P], where=s9)
            vbuf = sb("vbuf", [P, 2, GRP, D], where=s9)
            ga = sb("ga", [P, GRP, NT], where=s9)
            wg = sb("wg", [P, 2, GRP, NT], where=s9)
            ab9 = [ps(f"a9_{i}", s9) for i in range(GRP)]
            vb9 = [ps(f"v9_{i}", s9) for i in range(4)]
            u_full = [sem(f"u_full{i}") for i in range(GRP)]
            u_ready = [sem(f"u_ready{i}") for i in range(GRP)]
            e_full = [sem(f"e_full{i}") for i in range(2)]
            (g_hot, g_eq, g_b, g_mm, g_out, gelu_done, weighted, v_ready, acc_done) = map(sem, (
                "g_hot", "g_eq", "g_b", "g_mm", "g_out", "gelu_done", "weighted", "v_ready9", "acc9"))
            for half in range(2):
                g0 = half * NGH
                gb = half * (NT // 8)
                with nc.Block() as block:
                    @block.sync
                    def _(sp):
                        def u_load(g, s):
                            sp.wait_ge(u_ready[s], g)
                            sp.dma_start(ub[:, s], t["u"][g * GRP + s].rearrange("p (a b) -> p a b", a=KD)).then_inc(u_full[s], 16)

                        def v_load(g, p, wait):
                            if wait:
                                sp.wait_ge(v_ready, g * KD - KD)
                            sp.dma_start(vbuf[:, p], t["v"][bass.ds(g * GRP, GRP)].rearrange("g p n -> p g n")).then_inc(e_full[p], 16)
                        first = half == 0
                        for p in range(2):
                            for s in range(GRP):
                                u_load(g0 + p, s)
                            v_load(g0 + p, p, not first)
                        with sp.Fori(g0 // 2 + 1, (g0 + NGH) // 2) as i:
                            for p in range(2):
                                for s in range(GRP):
                                    u_load(i * 2 + p, s)
                                v_load(i * 2 + p, p, True)

                    @block.tensor
                    def _(pe):
                        def routing(n, p):
                            pe.wait_ge(g_hot, n + (gb + 1))
                            pe.wait_ge(g_b, n + (gb + 1))
                            for j in range(8):
                                mm = nc.tensor.matmul(ab9[p][:, j * HALF:(j + 1) * HALF], av[:, p, j], bv[:, p, j],
                                                      start=True, stop=True)
                            mm.then_inc(g_mm, 1)
                        routing(0, 0)
                        routing(1, 1)
                        with pe.Fori(1, NT // 16) as i:
                            for p in range(2):
                                pe.wait_ge(g_out, i * 2 + (p + gb - 1))
                                routing(i * 2 + p, p)
                        pe.wait_ge(g_out, NT // 8 + gb - 2)
                        routing(NT // 8 - 1, 0)
                        pe.wait_ge(g_out, gb + NT // 8)

                        def up(g, wait=True):
                            for s in range(GRP):
                                pe.wait_ge(u_full[s], 16 * g + 16)
                                if wait:
                                    pe.wait_ge(gelu_done, g * GRP + (s - GRP + 1))
                                for k in range(KD):
                                    mm = nc.tensor.matmul(ab9[s][:, 0:NT], ub[:, s, k], xn[:, k], start=(k == 0), stop=(k == KD - 1))
                                mm.then_inc(u_ready[s], 1)

                        def down(g, p, half_g, wait=True):
                            pe.wait_ge(e_full[p], 16 * half_g + 16)
                            pe.wait_ge(weighted, g * GRP + GRP)
                            for d in range(KD):
                                if wait or d >= 4:
                                    pe.wait_ge(acc_done, g * KD + (d - 3))
                                for s in range(GRP):
                                    mm = nc.tensor.matmul(vb9[d % 4][:, 0:NT], vbuf[:, p, s, d * P:(d + 1) * P], wg[:, p, s],
                                                          start=(s == 0), stop=(s == GRP - 1))
                                mm.then_inc(v_ready, 1)
                        up(g0, half > 0)
                        up(g0 + 1)
                        down(g0, 0, g0 // 2, half > 0)
                        with pe.Fori(g0 // 2, (g0 + NGH) // 2 - 1) as i:
                            up(i * 2 + 2)
                            down(i * 2 + 1, 1, i)
                            up(i * 2 + 3)
                            down(i * 2 + 2, 0, i + 1)
                        down(g0 + NGH - 1, 1, (g0 + NGH) // 2 - 1)

                    @block.scalar
                    def _(act):
                        def out(n, p):
                            act.wait_ge(g_mm, n + (gb + 1))
                            nc.scalar.copy(gw[:, bass.ds(n * 8, 8)].rearrange("p t k -> p (t k)"), ab9[p][:]).then_inc(g_out, 1)
                        with act.Fori(0, NT // 16) as i:
                            for p in range(2):
                                out(i * 2 + p, p)
                        out(NT // 8 - 1, 0)

                        def gelu(g, wait=True):
                            for s in range(GRP):
                                act.wait_ge(u_ready[s], g + 1)
                                if wait:
                                    act.wait_ge(weighted, g * GRP + (s - GRP + 1))
                                nc.scalar.activation(ga[:, s], ab9[s][:, 0:NT], ACT.Gelu).then_inc(gelu_done, 1)
                        gelu(g0, half > 0)
                        with act.Fori(g0 + 1, g0 + NGH) as g:
                            gelu(g)

                    @block.vector
                    def _(dve):
                        key = iota[:, half * HALF:(half + 1) * HALF]

                        def weigh_keys(n, p):
                            nc.vector.tensor_tensor(av[:, p], iota.unsqueeze(1).broadcast_to([P, 8, P]),
                                                    ig[:, 1, bass.ds(n * 8, 8)].unsqueeze(2).broadcast_to([P, 8, P]),
                                                    ALU.is_equal).then_inc(g_hot, 1)
                            nc.vector.tensor_tensor(bv[:, p], key.unsqueeze(1).broadcast_to([P, 8, HALF]),
                                                    ig[:, 0, bass.ds(n * 8, 8)].unsqueeze(2).broadcast_to([P, 8, HALF]),
                                                    ALU.is_equal).then_inc(g_eq, 1)
                            dve.wait_ge(g_eq, n + (gb + 1))
                            nc.vector.tensor_tensor(bv[:, p], bv[:, p], ig[:, 2, bass.ds(n * 8, 8)].unsqueeze(2).broadcast_to(
                                [P, 8, HALF]), ALU.mult).then_inc(g_b, 1)
                        weigh_keys(0, 0)
                        weigh_keys(1, 1)
                        with dve.Fori(1, NT // 16) as i:
                            for p in range(2):
                                dve.wait_ge(g_mm, i * 2 + (p + gb - 1))
                                weigh_keys(i * 2 + p, p)
                        dve.wait_ge(g_mm, NT // 8 + gb - 2)
                        weigh_keys(NT // 8 - 1, 0)
                        dve.wait_ge(g_out, gb + NT // 8)

                        def weigh(g, p, wait=True):
                            if wait:
                                dve.wait_ge(v_ready, g * KD - KD)
                            for s in range(GRP):
                                dve.wait_ge(gelu_done, g * GRP + (s + 1))
                                nc.vector.tensor_tensor(wg[:, p, s], ga[:, s], gw[:, :, g * GRP + (s - half * HALF)],
                                                        ALU.mult).then_inc(weighted, 1)

                        def add(g):
                            for d in range(KD):
                                dve.wait_ge(v_ready, g * KD + (d + 1))
                                nc.vector.tensor_tensor(res[:, d], res[:, d], vb9[d % 4][:, 0:NT], ALU.add).then_inc(acc_done, 1)
                        weigh(g0, 0, half > 0)
                        weigh(g0 + 1, 1, half > 0)
                        add(g0)
                        with dve.Fori(g0 // 2, (g0 + NGH) // 2 - 1) as i:
                            weigh(i * 2 + 2, 0)
                            add(i * 2 + 1)
                            weigh(i * 2 + 3, 1)
                            add(i * 2 + 2)
                        add(g0 + NGH - 1)
                        dve.wait_ge(acc_done, (g0 + NGH) * KD)

        with ExitStack() as s10:
            sq = sb("sq10", [P, KD, NT], where=s10)
            sb10 = ps("sum10", s10)
            sq10, sum10, var10, root10, y_done10 = map(sem, ("sq10", "sum10", "var10", "root10", "y_done10"))
            with nc.Block() as block:
                @block.scalar
                def _(act):
                    nc.scalar.activation(sq[:], res[:], ACT.Square).then_inc(sq10, 1)
                    act.wait_ge(var10, 1)
                    nc.scalar.activation(rstd[:, 0], rstd[:, 0], ACT.Sqrt).then_inc(root10, 1)

                @block.tensor
                def _(pe):
                    pe.wait_ge(sq10, 1)
                    for k in range(KD):
                        mm = nc.tensor.matmul(sb10[:, 0:NT], ones, sq[:, k], start=(k == 0), stop=(k == KD - 1))
                    mm.then_inc(sum10, 1)

                @block.vector
                def _(dve):
                    link = chain(dve, "c_ten")
                    dve.wait_ge(sum10, 1)
                    link(nc.vector.tensor_scalar(rstd[:, 1], sb10[:, 0:NT], 1.0 / D, EPS, ALU.mult, ALU.add))
                    nc.vector.reciprocal(rstd[:, 0], rstd[:, 1]).then_inc(var10, 1)
                    dve.wait_ge(root10, 1)
                    for k in range(KD):
                        nc.vector.scalar_tensor_tensor(out=xn[:, k], in0=res[:, k], scalar=par[:, P_GFIN + k:P_GFIN + k + 1],
                                                       in1=rstd[:, 0], op0=ALU.mult, op1=ALU.mult).then_inc(y_done10, 1)

                @block.sync
                def _(sp):
                    sp.wait_ge(y_done10, KD)
                    store(sp, t["y_out"], xn[:])
                    sp.wait_ge(out_done, 16 * outs[0])


def kernel(**inputs):
    import concourse.bacc as _bacc
    from concourse.bass_utils import run_bass_kernel_spmd as _run

    x = {k: np.asarray(v) for k, v in inputs.items()}
    n_pool = x["cache_k"].shape[1]
    col = lambda a: np.ascontiguousarray(a.reshape(-1, P).T)
    feat = lambda a: a.T.reshape(-1, P, a.shape[0]).transpose(1, 0, 2)
    w_in = x["w_in"][0]
    tiles = lambda w: w.reshape(-1, P, w.shape[1] // P, P).transpose(2, 1, 0, 3)
    w_out = tiles(x["w_out"][0]).reshape(KD, P, 2, D).transpose(0, 2, 1, 3).reshape(N_OUT, P, D)
    cst, sel = constants()
    par = np.zeros((P, P_ALL), np.float32)
    for at, v in ((P_GMIX, col(x["g_mix"][0])), (P_CB, col(x["conv_b"][0])), (P_DSK, col(np.repeat(x["d_skip"][0], HD))),
                  (P_GAT, col(x["g_attn"][0])), (P_GSSD, col(x["g_ssd"][0])), (P_GFFN, col(x["g_ffn"][0])),
                  (P_GFIN, col(x["g_final"])),
                  (P_CW, x["conv_w"][0].T.reshape(CONV_CH, P, CONV_W).transpose(1, 0, 2).reshape(P, -1))):
        par[:, at:at + v.shape[1]] = v
    par[0:NH, P_DTB], par[0:NH, P_ALOG] = x["dt_bias"][0], x["a_log"][0]
    ins = {
        "x": feat(np.concatenate([x["x_prompt"][0], x["x_sample"][:, 0]])),
        "cst": cst, "sel": sel, "par": par,
        "w_dt": w_in[:, PROJ * P:].reshape(KD, P, NH).transpose(1, 0, 2),
        "w_ring": np.concatenate([tiles(w_in[:, :PROJ * P]).reshape(N_IN, P, D), w_out,
                                  tiles(x["peer_wq"][0]).reshape(N_Q, P, D)]),
        "keys": x["peer_keys"][0].reshape(2 * PH, NKEY, P).transpose(2, 0, 1),
        "state_conv": x["state_conv"][0].reshape(NB, CONV_W - 1, CONV_CH, P).transpose(3, 2, 0, 1),
        "state_ssm": x["state_ssm"][0].reshape(NB, KD, P, P).transpose(2, 1, 0, 3),
        "page_table": x["page_table"].astype(np.int32).reshape(1, -1),
        "cache_k": x["cache_k"][0].reshape(n_pool, PAGE, KD, P).transpose(0, 3, 2, 1).reshape(n_pool, P, D),
        "cache_v": x["cache_v"][0].reshape(n_pool, PAGE, D),
        "u": x["peer_u"][0].reshape(NKEY, P, KD, P).transpose(0, 3, 2, 1).reshape(NKEY, P, D),
        "v": x["peer_v"][0].reshape(NKEY, P, D),
    }
    outs = {"y_out": (P, KD, NT), "k_out": (P, KD, NT), "v_out": (P, KD, NT), "conv_p": (P, CONV_CH, CONV_W - 1),
            "conv_s": (P, CONV_CH, NB, CONV_W - 1), "ssm_p": (P, KD, P), "ssm_s": (P, KD, NB, P)}
    nc = _bacc.Bacc("TRN2", target_bir_lowering=False, num_devices=1)
    t = {"n_pool": n_pool}
    arrays = {}
    for name, a in ins.items():
        a = np.ascontiguousarray(a)
        arrays[f"in_{name}"] = a
        t[name] = nc.dram_tensor(f"in_{name}", a.shape, mybir.dt.from_np(a.dtype), kind="ExternalInput").ap()
    for name, shape in outs.items():
        t[name] = nc.dram_tensor(f"out_{name}", shape, F32, kind="ExternalOutput").ap()
    build(nc, t)
    r = _run(nc, [arrays], core_ids=[0]).results[0]
    tok = {n: np.asarray(r[f"out_{n}"]).transpose(2, 1, 0).reshape(NT, D) for n in ("y_out", "k_out", "v_out")}
    heads = lambda a: (a[:TP].reshape(1, 1, TP, NH, HD), a[TP:].reshape(1, NB, 1, NH, HD))
    k_p, k_s = heads(tok["k_out"])
    v_p, v_s = heads(tok["v_out"])
    conv_p = np.asarray(r["out_conv_p"]).transpose(2, 1, 0).reshape(1, 1, CONV_W - 1, -1)
    conv_s = np.asarray(r["out_conv_s"]).transpose(2, 3, 1, 0).reshape(1, NB, CONV_W - 1, -1)
    ssm_p = np.asarray(r["out_ssm_p"]).transpose(1, 2, 0).reshape(1, 1, NH, HD, P)
    ssm_s = np.asarray(r["out_ssm_s"]).transpose(2, 1, 0, 3).reshape(1, NB, NH, HD, P)
    c = np.ascontiguousarray
    return (c(tok["y_out"][:TP].reshape(1, TP, D)), c(tok["y_out"][TP:].reshape(NB, 1, D)), c(k_p), c(v_p), c(k_s), c(v_s),
            c(conv_p), c(conv_s), c(ssm_p), c(ssm_s))
```

```python
from contextlib import ExitStack

import numpy as np

import concourse.bass as bass
from concourse import mybir

ALU = mybir.AluOpType
ACT = mybir.ActivationFunctionType
F32 = mybir.dt.float32
F32R = mybir.dt.float32r
U32 = mybir.dt.uint32
I32 = mybir.dt.int32
AX_X = mybir.AxisListType.X

P = 128
D = 1024
KD = D // P
TP = 256
NB = 8
NT = TP + NB
TT = TP // P
TILES = TT + 1
HD = 64
NH = 16
PAST = 256
PAGE = 128
NPG = PAST // PAGE
ROT = HD // 4
GROUPS = 2
CONV_W = 4
CONV_CH = 12
Q0, K0, V0, Z0, X0 = 0, KD, 2 * KD, 3 * KD, 4 * KD
B0, C0 = X0 + KD, X0 + KD + GROUPS
PROJ = 4 * KD + CONV_CH
MIXC = 2 * KD
PH = 8
NKEY = 128
TOPK = 16
RING = 4
N_IN, N_OUT, N_Q = PROJ, KD * MIXC // KD, 2 * PH
EPS = 1e-6
SCALE = HD ** -0.5
NEG = -1e30
HALF = NKEY // 2
GRP = 4
NG = NKEY // GRP
PIECE = 4 * P
RAW = 8
HL = 4
NPIECE = 2 * NKEY * D // PIECE
TG = 8
NTG = NT // TG

C_ID, C_ONE, C_IOTA, C_LAST, C_ROPC, C_ROPS, C_AM, C_CM = np.cumsum([0, P, P, P, P, NT, NT, 3 * P]).tolist()
C_SWAP = C_LAST
C_ALL = C_CM + P
(P_GMIX, P_CW, P_CB, P_DSK, P_GAT, P_GSSD, P_GFFN, P_GFIN, P_DTB, P_ALOG) = np.cumsum(
    [0, KD, CONV_CH * CONV_W, CONV_CH, KD, KD, KD, KD, KD, 1]).tolist()
P_ALL = P_ALOG + 1


def constants():
    c = np.zeros((P, C_ALL), np.float32)
    c[:, C_ID:C_ID + P] = np.eye(P)
    c[:, C_ONE:C_ONE + P] = 1.0
    half = ROT // 2
    inv = (np.float32(500000.0) ** (-np.arange(half, dtype=np.float32) / np.float32(half))).astype(np.float32)
    pos = np.concatenate([np.arange(TP), np.full(NB, PAST)]).astype(np.float32)
    ang = (pos[:, None] * inv[None, :]).astype(np.float32).T
    c[:, C_ROPC:C_ROPC + NT] = 1.0
    for h in (0, HD):
        for r in range(half):
            c[h + r, C_SWAP + h + half + r] = c[h + half + r, C_SWAP + h + r] = 1.0
            c[h + r, C_ROPC:C_ROPC + NT] = c[h + half + r, C_ROPC:C_ROPC + NT] = np.cos(ang[r])
            c[h + r, C_ROPS:C_ROPS + NT] = -np.sin(ang[r])
            c[h + half + r, C_ROPS:C_ROPS + NT] = np.sin(ang[r])
    i = np.arange(P)
    later = np.where(i[None, :] > i[:, None], np.float32(NEG), np.float32(0))
    c[:, C_AM:C_AM + P] = later
    c[:, C_AM + 2 * P:C_AM + 3 * P] = later
    c[:, C_CM:C_CM + P] = i[None, :] >= i[:, None]
    c[:, C_IOTA:C_IOTA + P] = i[None, :]
    sel = np.zeros((NH, KD, P), np.float32)
    for ch in range(KD):
        for p in range(P):
            sel[2 * ch + p // HD, ch, p] = 1.0
    return c, sel


def build(nc, t):
    ctx = ExitStack()
    with ctx:
        def sb(name, shape, dt=F32, where=ctx):
            return where.enter_context(nc.sbuf_tensor(name, shape, dt))

        def ps(name, where, shape=(P, 512)):
            return where.enter_context(nc.psum_tensor(name, list(shape), F32))

        stage_sems = []

        def sem(name):
            stage_sems.append(nc.alloc_semaphore(name=name))
            return stage_sems[-1]

        def lasting(name):
            return nc.alloc_semaphore(name=name)

        def recycle():
            nc.clear_and_free_semaphores(list(stage_sems))
            stage_sems.clear()
            nc.all_engine_barrier()

        cst = sb("cst", [P, C_LAST])
        par = sb("par", [P, P_ALL])
        ring = sb("ring", [P, RING, KD, P])
        res = sb("res", [P, KD, NT])
        rffn = sb("rffn", [P, NT])
        ig = sb("ig", [P, 3, NT])
        split = sb("split", [P, 2, KD, NT], F32R)
        ident = cst[:, C_ID:C_ID + P]
        ones = cst[:, C_ONE:C_ONE + P]
        iota = cst[:, C_IOTA:C_IOTA + P]

        ring_full = [lasting(f"ring_full{s}") for s in range(RING)]
        ring_used = [lasting(f"ring_used{s}") for s in range(RING)]

        def chain(eng, name):
            s, n = sem(name), [0]

            def link(*ins):
                for x in ins:
                    x.then_inc(s, 1)
                n[0] += len(ins)
                eng.wait_ge(s, n[0])
            return link

        def chain_loop(eng, s, base):
            n = [0]

            def link(*ins):
                for x in ins:
                    x.then_inc(s, 1)
                n[0] += len(ins)
                eng.wait_ge(s, base + n[0])
            return link

        def opened(eng, *sems):
            for s in sems:
                eng.sem_inc(s, 1)

        def load_ring(sp, i):
            for s in range(RING):
                sp.wait_ge(ring_used[s], i + 1)
                sp.dma_start(ring[:, s], t["w_ring"][i * RING + s].rearrange("p (a b) -> p a b", a=KD)
                             ).then_inc(ring_full[s], 16)

        st = ctx.enter_context(ExitStack())
        cmx = sb("cmx", [P, C_ALL - C_LAST], where=st)
        swap, rope_c, rope_s, amask, cmask = (
            cmx[:, at - C_LAST:at - C_LAST + n]
            for at, n in ((C_SWAP, P), (C_ROPC, NT), (C_ROPS, NT), (C_AM, 3 * P), (C_CM, P)))
        xn = sb("xn", [P, KD, NT], where=st)
        rstd = sb("rstd", [P, 2, NT], where=st)
        mix = sb("mix", [P, MIXC, NT], where=st)
        proj = sb("proj", [P, PROJ, NT], where=st)
        wdt = sb("wdt", [P, KD, NH], where=st)
        dth = sb("dth", [NH, NT], where=st)
        with ExitStack() as s1:
            sq = sb("sq1", [P, KD, NT], where=s1)
            bank = [ps(f"pj{i}", s1) for i in range(RING)]
            sumb = ps("sum1", s1)
            dtb = ps("dt1", s1)
            loaded, squared, summed, root_in, rooted, normed = map(sem, (
                "in_loaded", "in_squared", "in_summed", "in_root_in", "in_rooted", "in_normed"))
            pj_copied = [sem(f"pj_copied{i}") for i in range(RING)]
            dt_ready, dt_copied = sem("dt_ready"), sem("dt_copied")
            with nc.Block() as block:
                @block.sync
                def _(sp):
                    with sp.Fori(0, N_IN // RING + 1) as i:
                        load_ring(sp, i)

                @block.scalar
                def _(act):
                    opened(act, pj_copied[0], pj_copied[2])
                    for dst, src in ((res[:], t["x"]), (cst[:], t["cst"][:, 0:C_LAST]), (cmx[:], t["cst"][:, C_LAST:C_ALL]), (par[:], t["par"]), (wdt[:], t["w_dt"])):
                        act.dma_start(dst, src).then_inc(loaded, 16)
                    act.wait_ge(loaded, 80)
                    nc.scalar.activation(sq[:], res[:], ACT.Square).then_inc(squared, 1)
                    act.wait_ge(root_in, 1)
                    nc.scalar.activation(rstd[:, 0], rstd[:, 0], ACT.Sqrt).then_inc(rooted, 1)
                    with act.Fori(0, N_IN // RING) as i:
                        for s in (0, 2):
                            act.wait_ge(ring_used[s], i + 2)
                            nc.scalar.copy(proj[:, i * RING + s, :], bank[s][:, 0:NT]).then_inc(pj_copied[s], 1)
                    act.wait_ge(dt_ready, 1)
                    nc.scalar.copy(dth[:], dtb[0:NH, 0:NT]).then_inc(dt_copied, 1)
                    act.wait_ge(dt_copied, 1)

                @block.tensor
                def _(pe):
                    opened(pe, *ring_used)
                    pe.wait_ge(squared, 1)
                    for k in range(KD):
                        mm = nc.tensor.matmul(sumb[:, 0:NT], ones, sq[:, k], start=(k == 0), stop=(k == KD - 1))
                    mm.then_inc(summed, 1)
                    pe.wait_ge(normed, KD)
                    with pe.Fori(0, N_IN // RING) as i:
                        for s in range(RING):
                            pe.wait_ge(ring_full[s], 16 * i + 16)
                            pe.wait_ge(pj_copied[s], i + 1)
                            for k in range(KD):
                                mm = nc.tensor.matmul(bank[s][:, 0:NT], ring[:, s, k], xn[:, k],
                                                      start=(k == 0), stop=(k == KD - 1))
                            mm.then_inc(ring_used[s], 1)
                    for k in range(KD):
                        mm = nc.tensor.matmul(dtb[0:NH, 0:NT], wdt[:, k], xn[:, k], start=(k == 0), stop=(k == KD - 1))
                    mm.then_inc(dt_ready, 1)

                @block.vector
                def _(dve):
                    opened(dve, pj_copied[1], pj_copied[3])
                    link = chain(dve, "c_norm1")
                    dve.wait_ge(loaded, 80)
                    dve.wait_ge(summed, 1)
                    link(nc.vector.tensor_scalar(rstd[:, 1], sumb[:, 0:NT], 1.0 / D, EPS, ALU.mult, ALU.add))
                    nc.vector.reciprocal(rstd[:, 0], rstd[:, 1]).then_inc(root_in, 1)
                    dve.wait_ge(rooted, 1)
                    for k in range(KD):
                        nc.vector.scalar_tensor_tensor(out=xn[:, k], in0=res[:, k], scalar=par[:, P_GMIX + k:P_GMIX + k + 1],
                                                       in1=rstd[:, 0], op0=ALU.mult, op1=ALU.mult).then_inc(normed, 1)
                    with dve.Fori(0, N_IN // RING) as i:
                        for s in (1, 3):
                            dve.wait_ge(ring_used[s], i + 2)
                            nc.vector.tensor_copy(proj[:, i * RING + s, :], bank[s][:, 0:NT]).then_inc(pj_copied[s], 1)

        conv_s = sb("conv_s", [P, CONV_CH, NB, CONV_W], where=st)
        acs = sb("acs", [NH, TP], where=st)
        tokh = sb("tokh", [P, TT, 3, NH], where=st)
        dd = sb("dd", [NH, 2, NB], where=st)
        out_done = lasting("out_done")
        outs = [0]

        def store(eng, dst, src, n=1):
            outs[0] += n
            return eng.dma_start(dst, src).then_inc(out_done, 16)

        with ExitStack() as s2:
            cv = sb("cv", [P, CONV_CH, NT], where=s2)
            cs4 = sb("cs4", [P, CONV_CH, NB, CONV_W], where=s2)
            dtw = sb("dtw", [NH, 6, NT], where=s2)
            tps = ps("tps", s2)
            st_loaded, st_joined, acc_done, conv_done, silu_done = map(sem, (
                "conv_state", "conv_joined", "conv_acc", "conv_done", "silu_done"))
            raw_out = sem("raw_out")
            dt_a, dt_b, dt_c, dt_d, te_in, te_out, dec_in, acs_ready, tok_ready = map(sem, (
                "dt_abs", "dt_exp", "dt_one", "dt_log", "te_in", "te_out", "dec_in", "acs_ready", "tok_ready"))
            with nc.Block() as block:
                @block.sync
                def _(sp):
                    sp.dma_start(conv_s[:, :, :, 0:CONV_W - 1], t["state_conv"]).then_inc(st_loaded, 16)
                    sp.dma_start(t["conv_p"], proj[:, X0:X0 + CONV_CH, TP - 3:TP]).then_inc(raw_out, 16)
                    sp.wait_ge(raw_out, 16)

                @block.vector
                def _(dve):
                    link = chain(dve, "c_dt")
                    x, ab, e, u, w, q = (dtw[:, j] for j in range(6))
                    link(nc.vector.tensor_scalar(x, dth[:], par[0:NH, P_DTB:P_DTB + 1], None, ALU.add))
                    nc.vector.scalar_tensor_tensor(out=ab, in0=x, scalar=-1.0, in1=x, op0=ALU.mult, op1=ALU.max).then_inc(dt_a, 1)
                    dve.wait_ge(dt_b, 2)
                    nc.vector.tensor_scalar(u, e, 1.0, None, ALU.add).then_inc(dt_c, 1)
                    dve.wait_ge(dt_c, 1)
                    link(nc.vector.tensor_scalar(w, u, 1.0, None, ALU.subtract))
                    link(nc.vector.tensor_tensor(w, e, w, ALU.subtract), nc.vector.reciprocal(q, u))
                    link(nc.vector.tensor_tensor(w, w, q, ALU.mult))
                    dve.wait_ge(dt_d, 1)
                    link(nc.vector.tensor_tensor(w, w, ab, ALU.add))
                    link(nc.vector.scalar_tensor_tensor(out=dth[:], in0=x, scalar=0.0, in1=w, op0=ALU.max, op1=ALU.add))
                    link(nc.vector.tensor_scalar(u, dth[:], par[0:NH, P_ALOG:P_ALOG + 1], -1.0, ALU.mult, ALU.mult),
                         nc.vector.memset(q, 0.0))
                    for k in range(TT):
                        link(nc.vector.tensor_tensor_scan(acs[:, k * P:(k + 1) * P], u[:, k * P:(k + 1) * P],
                                                          q[:, k * P:(k + 1) * P], 0.0, ALU.add, ALU.add))
                    nc.vector.tensor_copy(dd[:, 0], u[:, TP:NT]).then_inc(dec_in, 1)
                    nc.vector.tensor_copy(dd[:, 1], dth[:, TP:NT]).then_inc(dec_in, 1)
                    for k in range(TT):
                        last = acs[:, (k + 1) * P - 1:(k + 1) * P]
                        nc.vector.tensor_scalar(x[:, k * P:(k + 1) * P], acs[:, k * P:(k + 1) * P], last, -1.0,
                                                ALU.subtract, ALU.mult).then_inc(te_in, 1)
                    dve.wait_ge(te_out, 2)
                    nc.vector.tensor_tensor(w[:, 0:TP], ab[:, 0:TP], dth[:, 0:TP], ALU.mult).then_inc(acs_ready, 1)
                    with dve.Fori(0, CONV_CH) as c:
                        cl = chain_loop(dve, acc_done, 4 * c)
                        cw = [par[:, bass.ds(c * CONV_W + (P_CW + j), 1)] for j in range(CONV_W)]
                        cl(nc.vector.tensor_scalar(cv[:, c, 0:TP], proj[:, c + X0, 0:TP], cw[3], None, ALU.mult))
                        for j in (1, 2, 3):
                            cl(nc.vector.scalar_tensor_tensor(out=cv[:, c, j:TP], in0=proj[:, c + X0, 0:TP - j],
                                                              scalar=cw[3 - j], in1=cv[:, c, j:TP], op0=ALU.mult, op1=ALU.add))
                    dve.wait_ge(st_loaded, 16)
                    nc.vector.tensor_copy(conv_s[:, :, :, 3], proj[:, X0:X0 + CONV_CH, TP:NT]).then_inc(st_joined, 1)
                    dve.wait_ge(st_joined, 1)
                    cwb = par[:, P_CW:P_CB].rearrange("p (c w) -> p c w", w=CONV_W).unsqueeze(2).broadcast_to(
                        [P, CONV_CH, NB, CONV_W])
                    link(nc.vector.tensor_tensor(cs4[:], conv_s[:], cwb, ALU.mult))
                    nc.vector.tensor_reduce(cv[:, :, TP:NT], cs4[:], AX_X, ALU.add).then_inc(conv_done, 1)
                    dve.wait_ge(tok_ready, 1)
                    nc.vector.tensor_copy(tokh[:].rearrange("p k j h -> p (k j h)"), tps[:, 0:TT * 3 * NH]).then_inc(acs_ready, 1)
                    dve.wait_ge(acs_ready, 2)

                @block.scalar
                def _(act):
                    act.wait_ge(dt_a, 1)
                    nc.scalar.activation(dtw[:, 2], dtw[:, 1], ACT.Exp, scale=-1.0).then_inc(dt_b, 1)
                    nc.scalar.activation(par[0:NH, P_ALOG:P_ALOG + 1], par[0:NH, P_ALOG:P_ALOG + 1], ACT.Exp).then_inc(dt_b, 1)
                    act.wait_ge(dt_c, 1)
                    nc.scalar.activation(dtw[:, 1], dtw[:, 3], ACT.Ln).then_inc(dt_d, 1)
                    act.wait_ge(dec_in, 2)
                    nc.scalar.activation(dd[:, 0], dd[:, 0], ACT.Exp).then_inc(te_out, 1)
                    act.wait_ge(te_in, TT)
                    nc.scalar.activation(dtw[:, 1, 0:TP], dtw[:, 0, 0:TP], ACT.Exp).then_inc(te_out, 1)
                    act.wait_ge(conv_done, 1)
                    act.wait_ge(raw_out, 16)
                    with act.Fori(0, CONV_CH) as c:
                        nc.scalar.activation(proj[:, c + X0, :], cv[:, c, :], ACT.Silu,
                                             bias=par[:, bass.ds(c + P_CB, 1)]).then_inc(silu_done, 1)
                    nc.scalar.activation(proj[:, Z0:Z0 + KD], proj[:, Z0:Z0 + KD], ACT.Silu).then_inc(silu_done, 1)
                    act.wait_ge(silu_done, CONV_CH + 1)

                @block.tensor
                def _(pe):
                    pe.wait_ge(acs_ready, 1)
                    for k in range(TT):
                        for j, src in enumerate((acs, dth, dtw[:, 4])):
                            at = (k * 3 + j) * NH
                            mm = nc.tensor.transpose(tps[:, at:at + NH], src[:, k * P:(k + 1) * P], cst[0:NH, C_ID:C_ID + NH])
                    mm.then_inc(tok_ready, 1)

        qkv_s = sb("qkv_s", [P, 3, KD, NB], where=st)
        with ExitStack() as s3:
            qk = sb("qk", [P, 2, NT], where=s3)
            tmp = sb("rtmp", [P, 2, NT], where=s3)
            vst = sb("vst", [P, TP], where=s3)
            vtok = sb("vtok", [P, TT, P], where=s3)
            sc = sb("scores", [P, 2, 3 * P], where=s3)
            pt = sb("probsT", [P, 2, 3 * P], where=s3)
            stat = sb("astat", [P, 2, 6], where=s3)
            sw, vb = ps("sw", s3), ps("vb", s3)
            sbk = [ps(f"s{j}", s3) for j in range(2)]
            ptb = [ps(f"pt{j}", s3) for j in range(2)]
            ob = [ps(f"o{j}", s3) for j in range(2)]
            (swapped, sw_free, rot, v_staged, v_turned, v_copied, qk_ready, k_out, s_ready, s_masked, maxed, expd, p_ready,
             p_turned, pt0_copied, pt1_copied, o_ready, o_copied, sam, summed3) = map(sem, (
                "swapped", "sw_free", "rot", "v_staged", "v_turned", "v_copied", "qk_ready", "k_out", "s_ready", "s_masked",
                "maxed", "expd", "p_ready", "p_turned", "pt0_copied", "pt1_copied", "o_ready", "o_copied", "sam", "rsum"))
            with nc.Block() as block:
                @block.sync
                def _(sp):
                    sp.dma_start(t["conv_s"], conv_s[:, :, :, 1:CONV_W]).then_inc(k_out, 16)
                    with sp.Fori(0, KD) as c:
                        sp.wait_ge(qk_ready, 2 * c + 2)
                        sp.dma_start(t["k_out"][:, c], qk[:, 1]).then_inc(k_out, 16)
                    sp.wait_ge(k_out, 16 * KD + 16)

                @block.tensor
                def _(pe):
                    opened(pe, s_ready, v_turned)
                    with pe.Fori(0, KD) as c:
                        for j, at in enumerate((Q0, K0)):
                            pe.wait_ge(sw_free, 2 * c + (j + 1))
                            nc.tensor.matmul(sw[:, 0:NT], swap, proj[:, c + at, :], start=True, stop=True).then_inc(swapped, 1)
                        pe.wait_ge(v_staged, c + 1)
                        pe.wait_ge(v_copied, c + 1)
                        for k in range(TT):
                            mm = nc.tensor.transpose(vb[:, k * P:(k + 1) * P], vst[:, k * P:(k + 1) * P], ident)
                        mm.then_inc(v_turned, 1)
                        pe.wait_ge(qk_ready, 2 * c + 2)
                        pe.wait_ge(o_copied, 2 * c + 1)
                        for j in range(2):
                            r = slice(j * HD, (j + 1) * HD)
                            nc.tensor.matmul(sbk[j][:, 0:P], qk[r, 0, 0:P], qk[r, 1, 0:P], start=True, stop=True)
                            nc.tensor.matmul(sbk[j][:, P:3 * P], qk[r, 0, P:TP], qk[r, 1, 0:TP],
                                             start=True, stop=True).then_inc(s_ready, 1)
                        for j in range(2):
                            pe.wait_ge(p_ready, 2 * c + j + 1)
                            nc.tensor.transpose(ptb[j][:, 0:P], sc[:, j, 0:P], ident)
                            nc.tensor.transpose(ptb[j][:, P:2 * P], sc[:, j, P:2 * P], ident)
                            nc.tensor.transpose(ptb[j][:, 2 * P:3 * P], sc[:, j, 2 * P:3 * P], ident).then_inc(p_turned, 1)
                        pe.wait_ge(v_copied, c + 2)
                        for j in range(2):
                            pe.wait_ge((pt0_copied, pt1_copied)[j], c + 1)
                            nc.tensor.matmul(ob[j][:, 0:P], vtok[:, 0], pt[:, j, 0:P], start=True, stop=True)
                            nc.tensor.matmul(ob[j][:, P:TP], vtok[:, 0], pt[:, j, P:2 * P], start=True, stop=False)
                            nc.tensor.matmul(ob[j][:, P:TP], vtok[:, 1], pt[:, j, 2 * P:3 * P], start=False,
                                             stop=True).then_inc(o_ready, 1)

                @block.vector
                def _(dve):
                    opened(dve, sw_free, v_copied)
                    with dve.Fori(0, KD) as c:
                        for j, at in enumerate((Q0, K0)):
                            if j == 1:
                                dve.wait_ge(k_out, 16 * c + 16)
                            else:
                                dve.wait_ge(s_ready, 2 * c + 1)
                            dve.wait_ge(swapped, 2 * c + j + 1)
                            nc.vector.tensor_tensor(tmp[:, 0], proj[:, c + at, :], rope_c, ALU.mult).then_inc(rot, 1)
                            nc.vector.tensor_tensor(tmp[:, 1], sw[:, 0:NT], rope_s, ALU.mult).then_inc(sw_free, 1)
                            dve.wait_ge(rot, 2 * c + j + 1)
                            dve.wait_ge(sw_free, 2 * c + (j + 2))
                            nc.vector.tensor_tensor(qk[:, j], tmp[:, 0], tmp[:, 1], ALU.add).then_inc(qk_ready, 1)
                            dve.wait_ge(qk_ready, 2 * c + j + 1)
                        dve.wait_ge(v_turned, c + 2)
                        nc.vector.tensor_copy(vtok[:].rearrange("p k f -> p (k f)"), vb[:, 0:TP]).then_inc(v_copied, 1)
                        sl = chain_loop(dve, s_masked, 6 * c)
                        for j in range(2):
                            dve.wait_ge(s_ready, 2 * c + (j + 2))
                            sl(nc.vector.tensor_tensor(sc[:, j], sbk[j][:, 0:3 * P], amask, ALU.add))
                            sl(nc.vector.tensor_reduce(stat[:, j, 0:1], sc[:, j, 0:P], AX_X, ALU.max),
                               nc.vector.tensor_reduce(stat[:, j, 1:2], sc[:, j, P:3 * P], AX_X, ALU.max))
                            nc.vector.tensor_scalar(stat[:, j, 0:2], stat[:, j, 0:2], -SCALE, None, ALU.mult).then_inc(maxed, 1)
                        for j in range(2):
                            dve.wait_ge(expd, 4 * c + 2 * j + 2)
                            nc.vector.reciprocal(stat[:, j, 4:6], stat[:, j, 2:4]).then_inc(summed3, 1)
                            dve.wait_ge(summed3, 2 * c + j + 1)
                            nc.vector.tensor_scalar(sc[:, j, 0:P], sc[:, j, 0:P], stat[:, j, 4:5], None, ALU.mult)
                            nc.vector.tensor_scalar(sc[:, j, P:3 * P], sc[:, j, P:3 * P], stat[:, j, 5:6], None,
                                                    ALU.mult).then_inc(p_ready, 1)
                        dve.wait_ge(p_turned, 2 * c + 2)
                        nc.vector.tensor_copy(pt[:, 1], ptb[1][:, 0:3 * P]).then_inc(pt1_copied, 1)

                @block.scalar
                def _(act):
                    opened(act, o_copied)
                    with act.Fori(0, KD) as c:
                        act.wait_ge(v_turned, c + 1)
                        nc.scalar.copy(vst[:], proj[:, c + V0, 0:TP]).then_inc(v_staged, 1)
                        nc.scalar.copy(qkv_s[:, 2, c, :], proj[:, c + V0, TP:NT]).then_inc(sam, 1)
                        act.wait_ge(qk_ready, 2 * c + 2)
                        nc.scalar.copy(qkv_s[:, 0:2, c, :], qk[:, :, TP:NT]).then_inc(sam, 1)
                        for j in range(2):
                            act.wait_ge(maxed, 2 * c + j + 1)
                            nc.scalar.activation(sc[:, j, 0:P], sc[:, j, 0:P], ACT.Exp, bias=stat[:, j, 0:1], scale=SCALE,
                                                 accum_out=stat[:, j, 2:3]).then_inc(expd, 1)
                            nc.scalar.activation(sc[:, j, P:3 * P], sc[:, j, P:3 * P], ACT.Exp, bias=stat[:, j, 1:2],
                                                 scale=SCALE, accum_out=stat[:, j, 3:4]).then_inc(expd, 1)
                        act.wait_ge(p_turned, 2 * c + 1)
                        nc.scalar.copy(pt[:, 0], ptb[0][:, 0:3 * P]).then_inc(pt0_copied, 1)
                        for j in range(2):
                            r = slice(j * HD, (j + 1) * HD)
                            act.wait_ge(o_ready, 2 * c + j + 1)
                            nc.scalar.copy(mix[r, c, 0:TP], ob[j][r, 0:TP]).then_inc(o_copied, 1)
                    act.wait_ge(o_copied, 2 * KD + 1)
                    act.wait_ge(sam, 2 * KD)

        with ExitStack() as s4:
            cb = sb("cb", [P, TT, GROUPS, P], where=s4)
            btok = sb("btok", [P, TT, GROUPS, P], where=s4)
            xst = sb("xst", [P, TP], where=s4)
            xtok = sb("xtok", [P, TT, P], where=s4)
            row = sb("row", [NH, 2, TP], where=s4)
            dec = sb("dec", [P, 2, TP], where=s4)
            wgt = sb("wgt", [P, 2, TP], where=s4)
            eb = sb("eb", [P, 2, P], where=s4)
            cs = sb("cs", [P, 2, P], where=s4)
            xw = sb("xw", [P, TT, P], where=s4)
            h0 = sb("h0", [P, P], where=s4)
            h1 = sb("h1", [P, P], where=s4)
            xb, hb0, hb1 = ps("xb", s4), ps("hb0", s4), ps("hb1", s4)
            bc = [ps(f"bc{j}", s4) for j in range(2)]
            yb = [ps(f"y{j}", s4) for j in range(2)]
            (cb_ready, cb_copied, x_staged, x_turned, x_copied, rows, bcd, d_ready, e_ready, eb_ready, w_ready, xw_ready,
             h0_ready, h0_copied, h1_ready, h1_done, h1_out, y_ready, y_done, cs_ready) = map(sem, (
                 "cb_ready", "cb_copied", "x_staged", "x_turned", "x_copied", "rows", "bcd", "d_ready", "e_ready", "eb_ready",
                 "w_ready", "xw_ready", "h0_ready", "h0_copied", "h1_ready", "h1_done", "h1_out", "y_ready", "y_done",
                 "cs_ready"))
            with nc.Block() as block:
                @block.sync
                def _(sp):
                    sp.dma_start(t["v_out"], proj[:, V0:V0 + KD]).then_inc(h1_out, 16)
                    with sp.Fori(0, KD) as c:
                        sp.wait_ge(h1_done, 2 * c + 3)
                        sp.dma_start(t["ssm_p"][:, c], h1[:]).then_inc(h1_out, 16)
                    sp.wait_ge(h1_out, 16 * KD + 16)

                @block.tensor
                def _(pe):
                    opened(pe, x_turned, y_ready, bcd, h1_ready)
                    for k in range(TT):
                        for g in range(GROUPS):
                            tk = slice(k * P, (k + 1) * P)
                            at = (k * GROUPS + g) * P
                            nc.tensor.matmul(bc[0][:, at:at + P], proj[:, B0 + g, tk], proj[:, C0 + g, tk], start=True, stop=True)
                            mm = nc.tensor.transpose(bc[1][:, at:at + P], proj[:, B0 + g, tk], ident)
                    mm.then_inc(cb_ready, 1)
                    pe.wait_ge(cb_copied, 2 * TT)
                    for g in range(GROUPS):
                        with pe.Fori(g * KD // GROUPS, (g + 1) * KD // GROUPS) as c:
                            pe.wait_ge(x_staged, c + 1)
                            for k in range(TT):
                                mm = nc.tensor.transpose(xb[:, k * P:(k + 1) * P], xst[:, k * P:(k + 1) * P], ident)
                            mm.then_inc(x_turned, 1)
                            for j in range(2):
                                pe.wait_ge(rows, 2 * c + j + 1)
                                nc.tensor.matmul(bc[j][:, 0:TP], cst[0:NH, C_ONE:C_ONE + P], row[:, j], start=True,
                                                 stop=True).then_inc(bcd, 1)
                            pe.wait_ge(xw_ready, 2 * c + 2)
                            pe.wait_ge(h0_copied, c + 1)
                            nc.tensor.matmul(hb0[:, 0:P], btok[:, 0, g], xw[:, 0], start=True, stop=True).then_inc(h0_ready, 1)
                            pe.wait_ge(h1_done, 2 * c + 1)
                            nc.tensor.matmul(hb1[:, 0:P], btok[:, 1, g], xw[:, 1], start=True, stop=True).then_inc(h1_ready, 1)
                            pe.wait_ge(h0_copied, c + 2)
                            pe.wait_ge(y_done, 2 * c + 1)
                            for j in range(2):
                                pe.wait_ge(w_ready, 4 * c + (2 * j + 3))
                                pe.wait_ge(cs_ready, 2 * c + j + 1)
                                nc.tensor.matmul(yb[j][:, 0:P], xtok[:, 0], wgt[:, j, 0:P], start=True, stop=True)
                                nc.tensor.matmul(yb[j][:, P:TP], xtok[:, 1], wgt[:, j, P:TP], start=True, stop=False)
                                nc.tensor.matmul(yb[j][:, P:TP], h0[:], cs[:, j], start=False, stop=True).then_inc(y_ready, 1)

                @block.scalar
                def _(act):
                    opened(act, h0_copied)
                    act.wait_ge(cb_ready, 1)
                    with act.Fori(0, KD) as c:
                        act.wait_ge(x_turned, c + 1)
                        nc.scalar.copy(xst[:], proj[:, c + X0, 0:TP]).then_inc(x_staged, 1)
                        for j in range(2):
                            act.wait_ge(bcd, 2 * c + (j + 2))
                            act.wait_ge(d_ready, 4 * c + 2 * j + 2)
                            act.wait_ge(h1_done, 2 * c + 1)
                            nc.scalar.activation(eb[:, j], bc[j][:, P:TP], ACT.Exp).then_inc(eb_ready, 1)
                            act.wait_ge(w_ready, 4 * c + 1)
                            nc.scalar.activation(dec[:, j], dec[:, j], ACT.Exp).then_inc(e_ready, 1)
                        act.wait_ge(h0_ready, c + 1)
                        act.wait_ge(y_ready, 2 * c + 1)
                        nc.scalar.copy(h0[:], hb0[:, 0:P]).then_inc(h0_copied, 1)

                @block.vector
                def _(dve):
                    opened(dve, h1_done, y_done, w_ready)
                    dve.wait_ge(cb_ready, 1)
                    for k in range(TT):
                        at = k * GROUPS * P
                        nc.vector.tensor_tensor(cb[:, k], bc[0][:, at:at + GROUPS * P].rearrange("p (g t) -> p g t", g=GROUPS),
                                                cmask.unsqueeze(1).broadcast_to([P, GROUPS, P]), ALU.mult).then_inc(cb_copied, 1)
                        nc.vector.tensor_copy(btok[:, k], bc[1][:, at:at + GROUPS * P].rearrange("p (g t) -> p g t", g=GROUPS)
                                              ).then_inc(cb_copied, 1)
                    dve.wait_ge(cb_copied, 2 * TT)
                    for g in range(GROUPS):
                        with dve.Fori(g * KD // GROUPS, (g + 1) * KD // GROUPS) as c:
                            for j in range(2):
                                dve.wait_ge(bcd, 2 * c + 1)
                                nc.vector.tensor_scalar(row[:, j], acs[:], cst[0:NH, bass.ds(c * 2 + j + C_ID, 1)], None,
                                                        ALU.mult).then_inc(rows, 1)
                            dve.wait_ge(x_turned, c + 2)
                            dve.wait_ge(y_ready, 2 * c + 1)
                            nc.vector.tensor_copy(xtok[:].rearrange("p k f -> p (k f)"), xb[:, 0:TP]).then_inc(x_copied, 1)
                            dve.wait_ge(x_copied, c + 1)
                            dve.wait_ge(h1_ready, c + 1)
                            for k in range(TT):
                                te = tokh[:, k, 2, bass.ds(c * 2, 2)].unsqueeze(2).broadcast_to([P, 2, HD])
                                nc.vector.tensor_tensor(xw[:, k].rearrange("p (j f) -> p j f", j=2),
                                                        xtok[:, k].rearrange("p (j f) -> p j f", j=2), te, ALU.mult
                                                        ).then_inc(xw_ready, 1)
                            for j in range(2):
                                dve.wait_ge(bcd, 2 * c + (j + 2))
                                for k in range(TT):
                                    nc.vector.tensor_scalar(dec[:, j, k * P:(k + 1) * P], bc[j][:, k * P:(k + 1) * P],
                                                            tokh[:, k, 0, bass.ds(c * 2 + j, 1)], 0.0, ALU.subtract, ALU.min
                                                            ).then_inc(d_ready, 1)
                            for j in range(2):
                                dve.wait_ge(e_ready, 2 * c + j + 1)
                                for k in range(TT):
                                    nc.vector.scalar_tensor_tensor(out=wgt[:, j, k * P:(k + 1) * P], in0=dec[:, j, k * P:(k + 1) * P],
                                                                   scalar=tokh[:, k, 1, bass.ds(c * 2 + j, 1)], in1=cb[:, k, g],
                                                                   op0=ALU.mult, op1=ALU.mult).then_inc(w_ready, 1)
                                dve.wait_ge(eb_ready, 2 * c + j + 1)
                                nc.vector.tensor_tensor(cs[:, j], eb[:, j], proj[:, C0 + g, P:TP], ALU.mult).then_inc(cs_ready, 1)
                            dve.wait_ge(h1_ready, c + 2)
                            dve.wait_ge(h0_copied, c + 2)
                            dve.wait_ge(h1_out, 16 * c + 16)
                            for j in range(2):
                                f = slice(j * HD, (j + 1) * HD)
                                nc.vector.scalar_tensor_tensor(out=h1[:, f], in0=h0[:, f], scalar=eb[:, j, P - 1:P], in1=hb1[:, f],
                                                               op0=ALU.mult, op1=ALU.add).then_inc(h1_done, 1)
                            for j in range(2):
                                r = slice(j * HD, (j + 1) * HD)
                                dve.wait_ge(y_ready, 2 * c + (j + 2))
                                nc.vector.scalar_tensor_tensor(out=mix[r, c + KD, 0:TP], in0=proj[r, c + X0, 0:TP],
                                                               scalar=par[r, bass.ds(c + P_DSK, 1)], in1=yb[j][r, 0:TP],
                                                               op0=ALU.mult, op1=ALU.add).then_inc(y_done, 1)
                    dve.wait_ge(y_done, 2 * KD + 1)

        recycle()
        with ExitStack() as s5:
            sel = sb("sel", [NH, KD, P], where=s5)
            hs = sb("hs", [P, KD, NB, P], where=s5)
            bcb = sb("bcb", [P, 2, GROUPS, NB, P], where=s5)
            ex = sb("ex", [P, 2, GROUPS, NB, P], where=s5)
            dds = sb("dds", [P, KD, 2, NB], where=s5)
            xdt = sb("xdt", [P, KD, NB], where=s5)
            u5 = sb("u5", [P, NB, P], where=s5)
            pb = [ps(f"b5_{i}", s5) for i in range(2 * GROUPS * NB * P // 512)]
            (h_loaded, ex_done, bc_done, bc_out, dd_done, xdt_done, c5, y5, hs_out, sel_loaded, hdec) = map(sem, (
                "h_loaded", "ex_done", "bc_done", "bc_out", "dd_done", "xdt_done", "c5", "y5", "hs_out", "sel_loaded", "hdec"))
            with nc.Block() as block:
                @block.sync
                def _(sp):
                    sp.dma_start(sel[:], t["sel"]).then_inc(sel_loaded, 16)
                    sp.dma_start(hs[:], t["state_ssm"]).then_inc(h_loaded, 16)
                    with sp.Fori(0, KD) as c:
                        sp.wait_ge(y5, c + 1)
                        sp.dma_start(t["ssm_s"][:, c], hs[:, c]).then_inc(hs_out, 16)
                    sp.wait_ge(hs_out, 16 * KD)

                @block.tensor
                def _(pe):
                    pe.wait_ge(sel_loaded, 16)
                    for c in range(KD):
                        mm = nc.tensor.matmul(pb[0][:, c * 2 * NB:(c + 1) * 2 * NB], sel[:, c], dd[:].rearrange("h a b -> h (a b)"),
                                              start=True, stop=True)
                    mm.then_inc(dd_done, 1)
                    pe.wait_ge(xdt_done, 1)
                    pe.wait_ge(ex_done, 2)
                    flat = ex[:].rearrange("p a g b n -> p (a g b n)")
                    for i, b in enumerate(pb):
                        nc.tensor.matmul(b[:], ones, flat[:, i * 512:(i + 1) * 512], start=True, stop=True).then_inc(bc_done, 1)

                @block.scalar
                def _(act):
                    flat = bcb[:].rearrange("p a g b n -> p (a g b n)")
                    for i, b in enumerate(pb):
                        act.wait_ge(bc_done, i + 1)
                        nc.scalar.copy(flat[:, i * 512:(i + 1) * 512], b[:]).then_inc(bc_out, 1)

                @block.gpsimd
                def _(pool):
                    pool.wait_ge(h_loaded, 16)
                    pool.wait_ge(xdt_done, 1)
                    with pool.Fori(0, KD) as c:
                        nc.gpsimd.tensor_tensor(hs[:, c], hs[:, c], dds[:, c, 0, :].unsqueeze(2).broadcast_to([P, NB, P]),
                                                ALU.mult).then_inc(hdec, 1)

                @block.vector
                def _(dve):
                    dve.wait_ge(dd_done, 1)
                    link = chain(dve, "c_five")
                    link(nc.vector.tensor_copy(dds[:].rearrange("p c a b -> p (c a b)"), pb[0][:, 0:KD * 2 * NB]))
                    nc.vector.tensor_tensor(xdt[:], proj[:, X0:X0 + KD, TP:NT], dds[:, :, 1], ALU.mult).then_inc(xdt_done, 1)
                    for a, at in enumerate((B0, C0)):
                        nc.vector.tensor_tensor(ex[:, a], ident.unsqueeze(1).unsqueeze(1).broadcast_to([P, GROUPS, NB, P]),
                                                proj[:, at:at + GROUPS, TP:NT].unsqueeze(3).broadcast_to([P, GROUPS, NB, P]),
                                                ALU.mult).then_inc(ex_done, 1)
                    dve.wait_ge(xdt_done, 1)
                    dve.wait_ge(bc_out, len(pb))
                    for g in range(GROUPS):
                        with dve.Fori(g * KD // GROUPS, (g + 1) * KD // GROUPS) as c:
                            cl = chain_loop(dve, c5, 4 * c)
                            cl(nc.vector.tensor_tensor(u5[:], bcb[:, 0, g], xdt[:, c].unsqueeze(2).broadcast_to([P, NB, P]),
                                                       ALU.mult))
                            dve.wait_ge(hdec, c + 1)
                            nc.vector.tensor_tensor(hs[:, c], hs[:, c], u5[:], ALU.add).then_inc(y5, 1)
                            dve.wait_ge(y5, c + 1)
                            cl(nc.vector.tensor_tensor(u5[:], hs[:, c], bcb[:, 1, g], ALU.mult))
                            cl(nc.vector.tensor_reduce(mix[:, c + KD, TP:NT], u5[:], AX_X, ALU.add))
                            cl(nc.vector.scalar_tensor_tensor(out=mix[:, c + KD, TP:NT], in0=proj[:, c + X0, TP:NT],
                                                              scalar=par[:, bass.ds(c + P_DSK, 1)], in1=mix[:, c + KD, TP:NT],
                                                              op0=ALU.mult, op1=ALU.add))


        with ExitStack() as s6:
            ptab = sb("ptab", [1, NB * NPG], I32, where=s6)
            kt = sb("kt", [P, 2, NPG, KD, PAGE], where=s6)
            vt = sb("vt", [P, 2, NPG, D], where=s6)
            qbd = sb("qbd", [P, NB, KD, 2], where=s6)
            pr = sb("pr", [P, NB, KD, 2], where=s6)
            st6 = sb("st6", [P, NPG * P], where=s6)
            p6 = sb("p6", [P, PAST + 1], where=s6)
            pts = sb("pts", [P, NPG + 1, P], where=s6)
            dg = sb("dg", [P, P], where=s6)
            a6 = sb("a6", [P, 4], where=s6)
            o6 = sb("o6", [P, KD, NB], where=s6)
            stb, ssb, ptb6, ob6 = (ps(n, s6) for n in ("stb", "ssb", "ptb6", "ob6"))
            (pt_loaded, zeroed, q_spread, st_copied, ss_ready, max6, exp6, sum6, p6_ready, dg_ready, pt6_ready,
             pts_ready, c6) = map(sem, (
                 "pt_loaded", "zeroed", "q_spread", "st_copied", "ss_ready", "max6", "exp6", "sum6", "p6_ready",
                 "dg_ready", "pt6_ready", "pts_ready", "c6"))
            k_full = [sem(f"k_full{s}") for s in range(2)]
            v_full = [sem(f"v_full{s}") for s in range(2)]
            k_used = [sem(f"k_used{s}") for s in range(2)]
            v_used = [sem(f"v_used{s}") for s in range(2)]
            with nc.Block() as block:
                @block.sync
                def _(sp):
                    sp.dma_start(ptab[:], t["page_table"]).then_inc(pt_loaded, 16)
                    sp.wait_ge(pt_loaded, 16)
                    for what, full, used in (("k", k_full, k_used), ("v", v_full, v_used)):
                        with sp.Fori(0, NB // 2) as i:
                            for s in range(2):
                                sp.wait_ge(used[s], i + 1)
                                for g in range(NPG):
                                    page = sp.value_load(ptab[0:1, bass.ds(i * (2 * NPG) + (s * NPG + g), 1)], min_val=0,
                                                         max_val=t["n_pool"] - 1)
                                    if what == "k":
                                        sp.dma_start(kt[:, s, g].rearrange("p c n -> p (c n)"),
                                                     t["cache_k"][bass.ds(page, 1)].rearrange("a p n -> p (a n)")
                                                     ).then_inc(full[s], 16)
                                    else:
                                        sp.dma_start(vt[:, s, g], t["cache_v"][bass.ds(page, 1)].rearrange("a p n -> p (a n)")
                                                     ).then_inc(full[s], 16)

                @block.tensor
                def _(pe):
                    opened(pe, *k_used, *v_used)
                    pe.wait_ge(q_spread, 4)
                    with pe.Fori(0, NB // 2) as i:
                        for s in range(2):
                            pe.wait_ge(k_full[s], 16 * NPG * i + 16 * NPG)
                            for g in range(NPG):
                                for c in range(KD):
                                    mm = nc.tensor.matmul(stb[:, bass.ds(i * (2 * NH) + (g * P + s * NH + 2 * c), 2)], kt[:, s, g, c],
                                                          qbd[:, i * 2 + s, c, :], start=True, stop=True)
                            mm.then_inc(k_used[s], 1)
                    pe.wait_ge(st_copied, 1)
                    for g in range(NPG):
                        nc.tensor.transpose(ssb[:, g * P:(g + 1) * P], st6[:, g * P:(g + 1) * P], ident)
                    nc.tensor.matmul(ssb[:, PAST:PAST + 1], pr[:].rearrange("p b c j -> p (b c j)"), ones[:, 0:1],
                                     start=True, stop=True).then_inc(ss_ready, 1)
                    pe.wait_ge(p6_ready, 1)
                    for g in range(NPG):
                        nc.tensor.transpose(ptb6[:, g * P:(g + 1) * P], p6[:, g * P:(g + 1) * P], ident)
                    pe.wait_ge(dg_ready, 1)
                    nc.tensor.matmul(ptb6[:, PAST:PAST + P], ones, dg[:], start=True, stop=True).then_inc(pt6_ready, 1)
                    pe.wait_ge(pts_ready, 1)
                    with pe.Fori(0, NB // 2) as i:
                        for s in range(2):
                            pe.wait_ge(v_full[s], 16 * NPG * i + 16 * NPG)
                            for c in range(KD):
                                for g in range(NPG):
                                    mm = nc.tensor.matmul(ob6[:, bass.ds(i * (2 * NH) + (s * NH + 2 * c), 2)],
                                                          vt[:, s, g, c * P:(c + 1) * P],
                                                          pts[:, g, bass.ds(i * (2 * NH) + (s * NH + 2 * c), 2)],
                                                          start=(g == 0), stop=(g == NPG - 1))
                            mm.then_inc(v_used[s], 1)

                @block.scalar
                def _(act):
                    act.wait_ge(max6, 1)
                    nc.scalar.activation(p6[:], ssb[:, 0:PAST + 1], ACT.Exp, bias=a6[:, 1:2], scale=SCALE,
                                         accum_out=a6[:, 2:3]).then_inc(exp6, 1)

                @block.vector
                def _(dve):
                    nc.vector.memset(qbd[:], 0.0).then_inc(zeroed, 1)
                    nc.vector.memset(pr[:], 0.0).then_inc(zeroed, 1)
                    dve.wait_ge(zeroed, 2)
                    for j in range(2):
                        r = slice(j * HD, (j + 1) * HD)
                        q, k = (qkv_s[r, n].rearrange("p c b -> p b c") for n in range(2))
                        nc.vector.tensor_copy(qbd[r, :, :, j], q).then_inc(q_spread, 1)
                        nc.vector.tensor_tensor(pr[r, :, :, j], q, k, ALU.mult).then_inc(q_spread, 1)
                    for s in range(2):
                        dve.wait_ge(k_used[s], NB // 2 + 1)
                    nc.vector.tensor_copy(st6[:], stb[:, 0:NPG * P]).then_inc(st_copied, 1)
                    dve.wait_ge(ss_ready, 1)
                    nc.vector.tensor_reduce(a6[:, 0:1], ssb[:, 0:PAST + 1], AX_X, ALU.max).then_inc(c6, 1)
                    dve.wait_ge(c6, 1)
                    nc.vector.tensor_scalar(a6[:, 1:2], a6[:, 0:1], -SCALE, None, ALU.mult).then_inc(max6, 1)
                    dve.wait_ge(exp6, 1)
                    nc.vector.reciprocal(a6[:, 3:4], a6[:, 2:3]).then_inc(sum6, 1)
                    dve.wait_ge(sum6, 1)
                    nc.vector.tensor_scalar(p6[:], p6[:], a6[:, 3:4], None, ALU.mult).then_inc(p6_ready, 1)
                    dve.wait_ge(p6_ready, 1)
                    nc.vector.tensor_scalar(dg[:], ident, p6[:, PAST:PAST + 1], None, ALU.mult).then_inc(dg_ready, 1)
                    dve.wait_ge(pt6_ready, 1)
                    nc.vector.tensor_copy(pts[:].rearrange("p g n -> p (g n)"), ptb6[:, 0:PAST + P]).then_inc(pts_ready, 1)
                    dve.wait_ge(pts_ready, 1)
                    for j in range(2):
                        r = slice(j * HD, (j + 1) * HD)
                        own = pts[r, NPG].rearrange("p (b c j) -> p j c b", b=NB, j=2)[:, j]
                        nc.vector.tensor_tensor(o6[r], qkv_s[r, 2], own, ALU.mult).then_inc(c6, 1)
                    dve.wait_ge(c6, 3)
                    for s in range(2):
                        dve.wait_ge(v_used[s], NB // 2 + 1)
                    for j in range(2):
                        r = slice(j * HD, (j + 1) * HD)
                        past = ob6[r, 0:P].rearrange("p (b c j) -> p j c b", b=NB, j=2)[:, j]
                        nc.vector.tensor_tensor(mix[r, 0:KD, TP:NT], past, o6[r], ALU.add).then_inc(c6, 1)
                    dve.wait_ge(c6, 5)

        with ExitStack() as s7:
            sq = sb("sq7", [P, MIXC, NT], where=s7)
            rr = sb("rr7", [P, 4, NT], where=s7)
            nb7 = [ps(f"n7_{i}", s7) for i in range(4)]
            ob7 = [ps(f"o7_{i}", s7) for i in range(2)]
            (gated, sq7, sum7, var7, root7, mixed, res_done, sq8, sum8, var8, root8) = map(sem, (
                "gated", "sq7", "sum7", "var7", "root7", "mixed", "res_done", "sq8", "sum8", "var8", "root8"))
            with nc.Block() as block:
                @block.sync
                def _(sp):
                    with sp.Fori(N_IN // RING + 1, (N_IN + N_OUT) // RING + 1) as i:
                        load_ring(sp, i)

                @block.scalar
                def _(act):
                    nc.scalar.activation(sq[:, 0:KD], mix[:, 0:KD], ACT.Square).then_inc(sq7, 1)
                    act.wait_ge(gated, 1)
                    nc.scalar.activation(sq[:, KD:MIXC], mix[:, KD:MIXC], ACT.Square).then_inc(sq7, 1)
                    act.wait_ge(var7, 1)
                    nc.scalar.activation(rr[:, 0:3], rr[:, 0:3], ACT.Sqrt).then_inc(root7, 1)
                    act.wait_ge(res_done, KD + 1)
                    nc.scalar.activation(sq[:, 0:KD], res[:], ACT.Square).then_inc(sq8, 1)
                    act.wait_ge(var8, 1)
                    nc.scalar.activation(rffn[:], rr[:, 3], ACT.Sqrt).then_inc(root8, 1)
                    act.wait_ge(root8, 1)

                @block.tensor
                def _(pe):
                    pe.wait_ge(sq7, 2)
                    for n, (a, b) in enumerate(((0, 8), (8, 12), (12, 16))):
                        for k in range(a, b):
                            mm = nc.tensor.matmul(nb7[n][:, 0:NT], ones, sq[:, k], start=(k == a), stop=(k == b - 1))
                    mm.then_inc(sum7, 1)
                    pe.wait_ge(mixed, MIXC)
                    with pe.Fori(0, N_OUT // RING) as i:
                        for m in range(2):
                            pe.wait_ge(res_done, i * 2 + 1)
                            for a in range(2):
                                s = 2 * m + a
                                pe.wait_ge(ring_full[s], 16 * i + 16 * (N_IN // RING + 1))
                                for k in range(KD):
                                    mm = nc.tensor.matmul(ob7[m][:, 0:NT], ring[:, s, k], mix[:, a * KD + k],
                                                          start=(a == 0 and k == 0), stop=(a == 1 and k == KD - 1))
                                mm.then_inc(ring_used[s], 1)
                    pe.wait_ge(sq8, 1)
                    for k in range(KD):
                        mm = nc.tensor.matmul(nb7[3][:, 0:NT], ones, sq[:, k], start=(k == 0), stop=(k == KD - 1))
                    mm.then_inc(sum8, 1)

                @block.vector
                def _(dve):
                    opened(dve, res_done)
                    link = chain(dve, "c_seven")
                    nc.vector.tensor_tensor(mix[:, KD:MIXC], mix[:, KD:MIXC], proj[:, Z0:Z0 + KD], ALU.mult).then_inc(gated, 1)
                    dve.wait_ge(sum7, 1)
                    link(*[nc.vector.tensor_scalar(rr[:, n], nb7[n][:, 0:NT], 1.0 / w, EPS, ALU.mult, ALU.add)
                           for n, w in enumerate((D, D // GROUPS, D // GROUPS))])
                    nc.vector.reciprocal(rr[:, 0:3], rr[:, 0:3]).then_inc(var7, 1)
                    dve.wait_ge(root7, 1)
                    for k in range(MIXC):
                        n = 0 if k < KD else 1 + (k - KD) // (KD // GROUPS)
                        nc.vector.scalar_tensor_tensor(out=mix[:, k], in0=mix[:, k], scalar=par[:, P_GAT + k:P_GAT + k + 1],
                                                       in1=rr[:, n], op0=ALU.mult, op1=ALU.mult).then_inc(mixed, 1)
                    with dve.Fori(0, KD // 2) as i:
                        for m in range(2):
                            dve.wait_ge(ring_used[2 * m + 1], i + (N_IN // RING + 2))
                            nc.vector.tensor_tensor(res[:, i * 2 + m, :], res[:, i * 2 + m, :], ob7[m][:, 0:NT],
                                                    ALU.add).then_inc(res_done, 1)
                    dve.wait_ge(sum8, 1)
                    link(nc.vector.tensor_scalar(rr[:, 3], nb7[3][:, 0:NT], 1.0 / D, EPS, ALU.mult, ALU.add))
                    nc.vector.reciprocal(rr[:, 3], rr[:, 3]).then_inc(var8, 1)
        st.close()

        recycle()
        HK = PH * TOPK
        N_U = NPIECE // 2
        MT = TT * P
        with ExitStack() as s8:
            acts = [sb("acts0", [P, HALF, NT], where=s8)]
            hl = sb("hl", [P, HL, 2, PIECE], F32R, where=s8)
            av = sb("av", [P, 2, TG, P], where=s8)
            bv = sb("bv", [P, 2, TG, HALF], where=s8)
            with ExitStack() as sk:
                xn = sb("xn8", [P, KD, NT], where=sk)
                keys = sb("keys", [P, 2 * PH, NKEY], where=sk)
                qst = sb("qst", [P, RING, NT], where=sk)
                scp = sb("scp", [P, 2 * PH, TT, NKEY], where=sk)
                scs = sb("scs", [NB, 2 * PH, NKEY], where=sk)
                scs2 = sb("scs2", [PH * NB, 2, NKEY], where=sk)
                stg = sb("stg", [P, 2, TT, NKEY], where=sk)
                rest = sb("rest", [P, TT, NKEY], where=sk)
                sv = sb("sv", [P, TT, 2, TOPK], where=sk)
                si = sb("si", [P, TT, 2, TOPK], U32, where=sk)
                cand = sb("cand", [P, TT, 2, TOPK * TOPK], where=sk)
                best = sb("best", [P, TT, TOPK], where=sk)
                bi = sb("bi", [P, TT, TOPK], U32, where=sk)
                sif = sb("sif", [P, TT, 2, PH + 1, TOPK], where=sk)
                bests = sb("bests", [P, TT, PH + 1, TOPK], where=sk)
                bis = sb("bis", [P, TT, PH + 1, TOPK], U32, where=sk)
                ab = sb("ab", [P, 2, TT, PH + 1, TOPK], U32, where=sk)
                abf = sb("abf", [P, 2, TT, PH + 1, TOPK], where=sk)
                rs = sb("rs8", [P, TT, PH + 1], where=sk)
                tick = sb("tick", [P, 2], where=sk)
                found = sb("found", [P, 3, TT, PH + 1, TOPK], where=sk)
                fsm = keys[0:NB, 0:3].rearrange("p n (h k) -> p n h k", h=PH)
            with ExitStack() as sk:
                acts.append(sb("acts1", [P, HALF, NT], where=sk))
            raw = ring[:].rearrange("p (a s) k n -> p (a s k n)", a=1).rearrange("p (r n) -> p r n", r=RAW)
            bank = [ps(f"bank{i}", s8) for i in range(8)]
            qb, scb, tb = bank[4:8], bank[2:4], bank[4:6]
            ub, rb, vb = bank[0:2], bank[2:4], bank[4:8]
            (keys_in, cleared, xn_done, x_split, best_done, sm_moved, eq_done, found_done, exp8, sub8, g_done, back, turned8,
             ig_done, steps) = map(sem, (
                 "keys_in", "cleared", "xn_done", "x_split", "best_done", "sm_moved", "eq_done", "found_done", "exp8", "sub8",
                 "g_done", "back", "turned8", "ig_done", "topk_steps"))
            q_copied = [sem(f"q_copied{i}") for i in range(RING)]
            sc_ready = [sem(f"sc_ready{i}") for i in range(2)]
            sc_copied = [sem(f"sc_copied{i}") for i in range(2)]
            raw_full = [sem(f"raw_full{i}") for i in range(RAW)]
            (hi_done, lo_done, used, gelu_done, g_eq, g_hot, g_b, g_mm, g_out, wg_hi, wg_done, acc_done) = map(sem, (
                "hi_done", "lo_done", "piece_used", "gelu_done", "g_eq", "g_hot", "g_b", "g_mm", "g_out", "wg_hi", "wg_done",
                "acc_done"))
            base = (N_IN + N_OUT) // RING
            order = [("q", 0), ("q", 1), ("s", 0), ("q", 2), ("s", 1), ("q", 3), ("s", 2), ("s", 3)]
            with nc.Block() as block:
                @block.sync
                def _(sp):
                    sp.dma_start(keys[:], t["keys"]).then_inc(keys_in, 16)
                    with sp.Fori(base + 1, base + N_Q // RING) as i:
                        load_ring(sp, i)
                    for r in range(RAW):
                        sp.wait_ge(ring_used[r // 2], base + N_Q // RING + 1)
                        sp.dma_start(raw[:, r], t["uv"][r]).then_inc(raw_full[r], 16)
                    for b in range(2):
                        sp.wait_ge(sc_copied[b], 4 * N_Q // RING + 1)
                    for h in range(PH):
                        sp.dma_start(scs2[h * NB:(h + 1) * NB], scs[:, 2 * h:2 * h + 2]).then_inc(sm_moved, 16)

                    def stream(first, end):
                        with sp.Fori(first, end) as i:
                            for r in range(RAW):
                                sp.wait_ge(lo_done, i * RAW + (r - RAW + 1))
                                sp.dma_start(raw[:, r], t["uv"][i * RAW + r]).then_inc(raw_full[r], 16)
                    stream(1, 4)
                    stream(4, N_U // RAW // 2)
                    sp.wait_ge(g_done, 2)
                    sp.wait_ge(found_done, 4)
                    for h in range(PH):
                        sp.dma_start(fsm[:, :, h], found[h * NB:(h + 1) * NB, :, 0, PH]).then_inc(back, 16)
                    stream(N_U // RAW // 2, NPIECE // RAW)

                @block.gpsimd
                def _(pool):
                    with pool.Fori(0, NPIECE // RAW) as i:
                        for r in range(RAW):
                            pool.wait_ge(hi_done, i * RAW + (r + 1))
                            nc.gpsimd.tensor_tensor(hl[:, r % HL, 1], raw[:, r], hl[:, r % HL, 0].bitcast(F32),
                                                    ALU.subtract).then_inc(lo_done, 1)

                @block.tensor
                def _(pe):
                    opened(pe, *sc_ready)
                    pe.wait_ge(keys_in, 16)
                    pe.wait_ge(xn_done, KD)
                    with pe.Fori(0, N_Q // RING) as i:
                        for kind, s in order:
                            if kind == "q":
                                pe.wait_ge(ring_full[s], 16 * i + 16 * (base + 1))
                                pe.wait_ge(q_copied[s], i + 1)
                                for k in range(KD):
                                    mm = nc.tensor.matmul(qb[s][:, 0:NT], ring[:, s, k], xn[:, k], start=(k == 0), stop=(k == KD - 1))
                                mm.then_inc(ring_used[s], 1)
                            else:
                                b = s % 2
                                pe.wait_ge(q_copied[s], i + 2)
                                pe.wait_ge(sc_copied[b], i * 4 + (2 * (s // 2) + 1))
                                for k in range(TILES):
                                    n = min(P, NT - k * P)
                                    mm = nc.tensor.matmul(scb[b][0:n, k * P:(k + 1) * P], qst[:, s, k * P:k * P + n],
                                                          keys[:, i * RING + s, :], start=True, stop=True)
                                mm.then_inc(sc_ready[b], 1)

                    def up(turn, j, wait=True):
                        out = ub[j % 2][:, 0:NT]
                        if wait:
                            pe.wait_ge(gelu_done, turn * 4 + (j - 1))
                        for a in range(2):
                            r = 2 * j + a
                            pe.wait_ge(lo_done, turn * RAW + (r + 1))
                            for k in range(4):
                                kk = 4 * a + k
                                tile = [hl[:, r % HL, m, k * P:(k + 1) * P] for m in range(2)]
                                for n, (m, x) in enumerate(((0, 0), (0, 1), (1, 0))):
                                    mm = nc.tensor.matmul(out, tile[m], split[:, x, kk], start=(kk == 0 and n == 0),
                                                          stop=(kk == KD - 1 and n == 2))
                            mm.then_inc(used, 1)

                    def route(m, p, done, wait=True):
                        if wait:
                            pe.wait_ge(g_out, m + (done - 1))
                        pe.wait_ge(g_b, m + (done + 1))
                        for j in range(TG):
                            mm = nc.tensor.matmul(rb[p][:, j * HALF:(j + 1) * HALF], av[:, p, j], bv[:, p, j], start=True, stop=True)
                        mm.then_inc(g_mm, 1)

                    def down(g, p, ds, first=False):
                        pe.wait_ge(wg_done, g * GRP + GRP)
                        for d in ds:
                            if not first or d >= 4:
                                pe.wait_ge(acc_done, g * KD + (d - 3))
                            pe.wait_ge(lo_done, g * RAW + (d + 1 + N_U))
                            out = vb[d % 4][:, 0:NT]
                            for s in range(GRP):
                                tile = [hl[:, d % HL, m, s * P:(s + 1) * P] for m in range(2)]
                                for n, (m, x) in enumerate(((0, 0), (0, 1), (1, 0))):
                                    mm = nc.tensor.matmul(out, tile[m], split[:, p, 2 * s + x], start=(s == 0 and n == 0),
                                                          stop=(s == GRP - 1 and n == 2))
                            mm.then_inc(used, 1)

                    pe.wait_ge(x_split, 3)
                    for j in range(4):
                        up(0, j, wait=j > 1)
                    with pe.Fori(1, NKEY // 8) as i:
                        for j in range(4):
                            up(i, j)
                    pe.wait_ge(found_done, 4)
                    pe.wait_ge(g_done, 2)
                    pe.wait_ge(back, 16 * PH)
                    for n in range(3):
                        if n == 2:
                            pe.wait_ge(ig_done, 1)
                        for k in range(TT):
                            nc.tensor.transpose(tb[n % 2][:, k * P:(k + 1) * P],
                                                found[:, n, k, 0:PH].rearrange("p h k -> p (h k)"), ident)
                        nc.tensor.transpose(tb[n % 2][:, MT:NT], fsm[:, n].rearrange("p h k -> p (h k)"), cst[0:NB, C_ID:C_ID + NB]
                                            ).then_inc(turned8, 1)
                    for j in range(4):
                        up(NKEY // 8, j)
                        if j % 2:
                            route(j // 2, j // 2, 0, wait=False)
                    with pe.Fori(1, NKEY // 8) as i:
                        for j in range(4):
                            up(i + NKEY // 8, j)
                            if j % 2:
                                route(i * 2 + j // 2, j // 2, 0)
                    route(NTG - 1, 0, 0)
                    for p in range(2):
                        down(p, p, range(4), first=p == 0)
                        route(2 * p, 0, NTG)
                        down(p, p, range(4, 8))
                        route(2 * p + 1, 1, NTG)
                    with pe.Fori(1, NG // 4) as i:
                        for p in range(2):
                            down(i * 2 + p, p, range(4))
                            route(i * 4 + 2 * p, 0, NTG)
                            down(i * 2 + p, p, range(4, 8))
                            route(i * 4 + (2 * p + 1), 1, NTG)
                    route(NTG - 1, 0, NTG)
                    with pe.Fori(NG // 4, NG // 2) as i:
                        for p in range(2):
                            down(i * 2 + p, p, range(8))

                @block.scalar
                def _(act):
                    opened(act, *q_copied, *sc_copied)
                    with act.Fori(0, N_Q // RING) as i:
                        for kind, s in order:
                            b = s % 2
                            if kind == "q":
                                act.wait_ge(ring_used[s], i + (base + 2))
                                act.wait_ge(sc_ready[b], i * 2 + 1)
                                nc.scalar.copy(qst[:, s], qb[s][:, 0:NT]).then_inc(q_copied[s], 1)
                            else:
                                act.wait_ge(sc_ready[b], i * 2 + (s // 2 + 2))
                                nc.scalar.copy(scp[:, i * RING + s].rearrange("p t n -> p (t n)"), scb[b][:, 0:TP]
                                               ).then_inc(sc_copied[b], 1)
                                nc.scalar.copy(scs[:, i * RING + s, :], scb[b][0:NB, TP:TP + P]).then_inc(sc_copied[b], 1)

                    def high(turn, r, wait=True):
                        act.wait_ge(raw_full[r], 16 * turn + 16)
                        if wait:
                            act.wait_ge(used, turn * RAW + (r - HL + 1))
                        nc.scalar.copy(hl[:, r % HL, 0], raw[:, r]).then_inc(hi_done, 1)

                    def gelu(turn, j, out):
                        act.wait_ge(used, turn * RAW + (2 * j + 2))
                        nc.scalar.activation(out, ub[j % 2][:, 0:NT], ACT.Gelu).then_inc(gelu_done, 1)
                    for r in range(HL):
                        high(0, r, wait=False)

                    def chunks(t0, t1, half):
                        with act.Fori(t0, t1) as i:
                            for j in range(4):
                                gelu(i, j, acts[half][:, i * 4 + (j - half * HALF), :])
                                for r in (2 * j + HL, 2 * j + HL + 1):
                                    high(i + r // RAW, r % RAW)
                    chunks(0, NKEY // 8 - 3, 0)
                    act.wait_ge(sub8, 1)
                    nc.scalar.activation(found[:, 2], found[:, 2], ACT.Exp).then_inc(exp8, 1)
                    chunks(NKEY // 8 - 3, NKEY // 8, 0)
                    act.wait_ge(ig_done, 3)
                    chunks(NKEY // 8, NKEY // 4, 1)
                    with act.Fori(N_U // RAW, NPIECE // RAW - 1) as i:
                        for r in range(HL, HL + RAW):
                            high(i + r // RAW, r % RAW)
                    for r in range(HL, RAW):
                        high(NPIECE // RAW - 1, r)

                @block.vector
                def _(dve):
                    for k in range(KD):
                        nc.vector.scalar_tensor_tensor(out=xn[:, k], in0=res[:, k], scalar=par[:, P_GFFN + k:P_GFFN + k + 1],
                                                       in1=rffn[:], op0=ALU.mult, op1=ALU.mult).then_inc(xn_done, 1)
                    dve.wait_ge(xn_done, KD)
                    nc.vector.tensor_copy(split[:, 0], xn[:]).then_inc(x_split, 1)
                    dve.wait_ge(x_split, 1)
                    nc.vector.tensor_tensor(split[:, 1], xn[:], split[:, 0].bitcast(F32), ALU.subtract).then_inc(x_split, 1)
                    nc.vector.memset(sif[:, :, :, PH], 0.0).then_inc(cleared, 1)
                    nc.vector.memset(bests[:, :, PH], 0.0).then_inc(cleared, 1)
                    nc.vector.memset(bis[:, :, PH], 0).then_inc(cleared, 1)
                    nc.vector.memset(tick[:], 0.0).then_inc(cleared, 1)
                    dve.wait_ge(cleared, 4)
                    nc.vector.tensor_copy(tick[:, 1:2], tick[:, 0:1]).then_inc(x_split, 1)
                    for b in range(2):
                        dve.wait_ge(sc_copied[b], 4 * N_Q // RING + 1)

                    def top16(link, tiles, src, spare, val, idx):
                        link(*[nc.vector.max(val(k)[:, 0:8], src(k)) for k in tiles])
                        link(*[nc.vector.max_index(idx(k)[:, 0:8], val(k)[:, 0:8], src(k)) for k in tiles])
                        link(*[nc.vector.match_replace(spare(k), val(k)[:, 0:8], src(k), -3e38) for k in tiles])
                        link(*[nc.vector.max(val(k)[:, 8:16], spare(k)) for k in tiles])
                        link(*[nc.vector.max_index(idx(k)[:, 8:16], val(k)[:, 8:16], spare(k)) for k in tiles])

                    def choose(link, n, tiles, src):
                        for side in range(2):
                            top16(link, tiles, lambda k: src(side, k), lambda k: rest[0:n, k],
                                  lambda k: sv[0:n, k, side], lambda k: si[0:n, k, side])
                        link(*[nc.vector.tensor_tensor(
                            cand[0:n, k, 0].rearrange("p (a b) -> p a b", a=TOPK),
                            sv[0:n, k, 0].unsqueeze(2).broadcast_to([n, TOPK, TOPK]),
                            sv[0:n, k, 1].unsqueeze(1).broadcast_to([n, TOPK, TOPK]), ALU.add) for k in tiles])
                        top16(link, tiles, lambda k: cand[0:n, k, 0], lambda k: cand[0:n, k, 1],
                              lambda k: best[0:n, k], lambda k: bi[0:n, k])

                    with dve.Fori(0, PH) as h:
                        nc.vector.tensor_copy(stg[:], scp[:, bass.ds(h * 2, 2)]).then_inc(eq_done, 1)
                        dve.wait_ge(eq_done, h + 1)
                        nc.vector.memset(tick[:, 0:1], 0.0)
                        dve.sem_clear(steps)
                        link = chain_loop(dve, steps, 0)
                        choose(link, P, range(TT), lambda side, k: stg[:, side, k])
                        nc.vector.tensor_copy(sif[:, :, :, h, :], si[:]).then_inc(best_done, 1)
                        nc.vector.tensor_copy(bests[:, :, h, :], best[:]).then_inc(best_done, 1)
                        nc.vector.tensor_copy(bis[:, :, h, :], bi[:]).then_inc(best_done, 1)
                        dve.wait_ge(best_done, h * 3 + 3)
                    hb = PH * NB
                    dve.wait_ge(sm_moved, 16 * PH)
                    nc.vector.memset(tick[:, 0:1], 0.0)
                    dve.sem_clear(steps)
                    link = chain_loop(dve, steps, 0)
                    choose(link, hb, range(1), lambda side, k: scs2[:, side])
                    link(nc.vector.tensor_copy(sif[0:hb, 0, :, PH], si[0:hb, 0]),
                         nc.vector.tensor_copy(bests[0:hb, 0, PH], best[0:hb, 0]),
                         nc.vector.tensor_copy(bis[0:hb, 0, PH], bi[0:hb, 0]))
                    w = found[:, 2]
                    nc.vector.tensor_tensor(w, bests[:], bests[:, :, :, 0:1].broadcast_to([P, TT, PH + 1, TOPK]),
                                            ALU.subtract).then_inc(sub8, 1)
                    link(nc.vector.tensor_single_scalar(ab[:, 0], bis[:], 4, ALU.logical_shift_right),
                         nc.vector.tensor_single_scalar(ab[:, 1], bis[:], 15, ALU.bitwise_and))
                    link(nc.vector.tensor_copy(abf[:], ab[:]))
                    eq = scp[:].rearrange("p a t n -> p (a t n)")
                    for side in range(2):
                        for k in range(TT):
                            e = eq[:, 0:(PH + 1) * TOPK * TOPK].rearrange("p (x a) -> p x a", a=TOPK)
                            link(nc.vector.tensor_tensor(
                                e, abf[:, side, k].rearrange("p h k -> p (h k)").unsqueeze(2).broadcast_to([P, (PH + 1) * TOPK, TOPK]),
                                iota[:, 0:TOPK].unsqueeze(1).broadcast_to([P, (PH + 1) * TOPK, TOPK]), ALU.is_equal))
                            e4 = eq[:, 0:(PH + 1) * TOPK * TOPK].rearrange("p (h k a) -> p h k a", h=PH + 1, k=TOPK)
                            link(nc.vector.tensor_tensor(e4, e4, sif[:, k, side].unsqueeze(2).broadcast_to([P, PH + 1, TOPK, TOPK]),
                                                         ALU.mult))
                            nc.vector.tensor_reduce(found[:, side, k].rearrange("p h k -> p (h k)"), e, AX_X, ALU.add
                                                    ).then_inc(found_done, 1)
                            dve.wait_ge(found_done, side * TT + k + 1)
                    dve.wait_ge(exp8, 1)
                    link(nc.vector.tensor_reduce(rs[:], w, AX_X, ALU.add))
                    nc.vector.reciprocal(rs[:], rs[:]).then_inc(g_done, 1)
                    dve.wait_ge(g_done, 1)
                    nc.vector.tensor_tensor(w, w, rs[:].unsqueeze(3).broadcast_to([P, TT, PH + 1, TOPK]), ALU.mult
                                            ).then_inc(g_done, 1)
                    for n in range(3):
                        dve.wait_ge(turned8, n + 1)
                        nc.vector.tensor_copy(ig[:, n], tb[n % 2][:, 0:NT]).then_inc(ig_done, 1)
                    dve.wait_ge(ig_done, 3)

                    def one_hots(m, p, half, wait=True):
                        done = half * NTG
                        if wait:
                            dve.wait_ge(g_mm, m + (done - 1))
                        key = iota[:, half * HALF:(half + 1) * HALF]
                        tok = [ig[:, n, bass.ds(m * TG, TG)].unsqueeze(2) for n in range(3)]
                        nc.vector.tensor_tensor(av[:, p], iota.unsqueeze(1).broadcast_to([P, TG, P]),
                                                tok[1].broadcast_to([P, TG, P]), ALU.is_equal)
                        nc.vector.tensor_tensor(bv[:, p], key.unsqueeze(1).broadcast_to([P, TG, HALF]),
                                                tok[0].broadcast_to([P, TG, HALF]), ALU.is_equal).then_inc(g_eq, 1)
                        dve.wait_ge(g_eq, m + (done + 1))
                        nc.vector.tensor_tensor(bv[:, p], bv[:, p], tok[2].broadcast_to([P, TG, HALF]), ALU.mult).then_inc(g_b, 1)

                    def weigh(m, p, half):
                        dve.wait_ge(g_mm, m + (half * NTG + 1))
                        a = acts[half][:, :, bass.ds(m * TG, TG)].rearrange("p c t -> p t c")
                        nc.vector.tensor_tensor(a, a, rb[p][:].rearrange("p (t c) -> p t c", t=TG), ALU.mult).then_inc(g_out, 1)

                    one_hots(0, 0, 0, wait=False)
                    one_hots(1, 1, 0, wait=False)
                    dve.wait_ge(gelu_done, HALF)
                    with dve.Fori(0, NTG // 2 - 1) as i:
                        for p in range(2):
                            weigh(i * 2 + p, p, 0)
                            one_hots(i * 2 + (p + 2), p, 0)
                    weigh(NTG - 3, 0, 0)
                    one_hots(NTG - 1, 0, 0)
                    weigh(NTG - 2, 1, 0)
                    weigh(NTG - 1, 0, 0)
                    dve.wait_ge(g_out, NTG)

                    def parts(g, p, half):
                        dve.wait_ge(used, g * RAW + (N_U - RAW))
                        for s in range(GRP):
                            a = acts[half][:, g * GRP + (s - half * HALF), :]
                            nc.vector.tensor_copy(split[:, p, 2 * s], a).then_inc(wg_hi, 1)
                            dve.wait_ge(wg_hi, g * GRP + (s + 1))
                            nc.vector.tensor_tensor(split[:, p, 2 * s + 1], a, split[:, p, 2 * s].bitcast(F32), ALU.subtract
                                                    ).then_inc(wg_done, 1)

                    def add(g, ds):
                        for d in ds:
                            dve.wait_ge(used, g * RAW + (d + 1 + N_U))
                            nc.vector.tensor_tensor(res[:, d], res[:, d], vb[d % 4][:, 0:NT], ALU.add).then_inc(acc_done, 1)

                    one_hots(0, 0, 1)
                    one_hots(1, 1, 1)
                    dve.wait_ge(used, N_U)
                    parts(0, 0, 0)
                    dve.wait_ge(gelu_done, NKEY)
                    with dve.Fori(0, NG // 4 - 1) as i:
                        for p in range(2):
                            g = i * 2 + p
                            parts(g + 1, 1 - p, 0)
                            for q in range(2):
                                add(g, range(4 * q, 4 * q + 4))
                                weigh(g * 2 + q, q, 1)
                                one_hots(g * 2 + (q + 2), q, 1)
                    g = NG // 2 - 2
                    parts(g + 1, 1, 0)
                    add(g, range(4))
                    weigh(NTG - 5, 0, 1)
                    one_hots(NTG - 3, 0, 1)
                    add(g, range(4, 8))
                    weigh(NTG - 4, 1, 1)
                    one_hots(NTG - 2, 1, 1)
                    add(g + 1, range(4))
                    weigh(NTG - 3, 0, 1)
                    one_hots(NTG - 1, 0, 1)
                    add(g + 1, range(4, 8))
                    weigh(NTG - 2, 1, 1)
                    weigh(NTG - 1, 0, 1)
                    dve.wait_ge(g_out, 2 * NTG)
                    parts(NG // 2, 0, 1)
                    with dve.Fori(NG // 4, NG // 2 - 1) as i:
                        for p in range(2):
                            parts(i * 2 + (p + 1), 1 - p, 1)
                            add(i * 2 + p, range(8))
                    parts(NG - 1, 1, 1)
                    add(NG - 2, range(8))
                    add(NG - 1, range(8))
                    dve.wait_ge(acc_done, NG * KD)

        with ExitStack() as s10:
            sq = sb("sq10", [P, KD, NT], where=s10)
            xn = sb("xn10", [P, KD, NT], where=s10)
            rstd = sb("rstd10", [P, 2, NT], where=s10)
            sb10 = ps("sum10", s10)
            sq10, sum10, var10, root10, y_done10 = map(sem, ("sq10", "sum10", "var10", "root10", "y_done10"))
            with nc.Block() as block:
                @block.scalar
                def _(act):
                    nc.scalar.activation(sq[:], res[:], ACT.Square).then_inc(sq10, 1)
                    act.wait_ge(var10, 1)
                    nc.scalar.activation(rstd[:, 0], rstd[:, 0], ACT.Sqrt).then_inc(root10, 1)

                @block.tensor
                def _(pe):
                    pe.wait_ge(sq10, 1)
                    for k in range(KD):
                        mm = nc.tensor.matmul(sb10[:, 0:NT], ones, sq[:, k], start=(k == 0), stop=(k == KD - 1))
                    mm.then_inc(sum10, 1)

                @block.vector
                def _(dve):
                    link = chain(dve, "c_ten")
                    dve.wait_ge(sum10, 1)
                    link(nc.vector.tensor_scalar(rstd[:, 1], sb10[:, 0:NT], 1.0 / D, EPS, ALU.mult, ALU.add))
                    nc.vector.reciprocal(rstd[:, 0], rstd[:, 1]).then_inc(var10, 1)
                    dve.wait_ge(root10, 1)
                    for k in range(KD):
                        nc.vector.scalar_tensor_tensor(out=xn[:, k], in0=res[:, k], scalar=par[:, P_GFIN + k:P_GFIN + k + 1],
                                                       in1=rstd[:, 0], op0=ALU.mult, op1=ALU.mult).then_inc(y_done10, 1)

                @block.sync
                def _(sp):
                    sp.wait_ge(y_done10, KD)
                    store(sp, t["y_out"], xn[:])
                    sp.wait_ge(out_done, 16 * outs[0])


def kernel(**inputs):
    import concourse.bacc as _bacc
    from concourse.bass_utils import run_bass_kernel_spmd as _run

    x = {k: np.asarray(v) for k, v in inputs.items()}
    n_pool = x["cache_k"].shape[1]
    col = lambda a: np.ascontiguousarray(a.reshape(-1, P).T)
    feat = lambda a: a.T.reshape(-1, P, a.shape[0]).transpose(1, 0, 2)
    w_in = x["w_in"][0]
    tiles = lambda w: w.reshape(-1, P, w.shape[1] // P, P).transpose(2, 1, 0, 3)
    w_out = tiles(x["w_out"][0]).reshape(KD, P, 2, D).transpose(0, 2, 1, 3).reshape(N_OUT, P, D)
    cst, sel = constants()
    par = np.zeros((P, P_ALL), np.float32)
    for at, v in ((P_GMIX, col(x["g_mix"][0])), (P_CB, col(x["conv_b"][0])), (P_DSK, col(np.repeat(x["d_skip"][0], HD))),
                  (P_GAT, col(x["g_attn"][0])), (P_GSSD, col(x["g_ssd"][0])), (P_GFFN, col(x["g_ffn"][0])),
                  (P_GFIN, col(x["g_final"])),
                  (P_CW, x["conv_w"][0].T.reshape(CONV_CH, P, CONV_W).transpose(1, 0, 2).reshape(P, -1))):
        par[:, at:at + v.shape[1]] = v
    par[0:NH, P_DTB], par[0:NH, P_ALOG] = x["dt_bias"][0], x["a_log"][0]
    ins = {
        "x": feat(np.concatenate([x["x_prompt"][0], x["x_sample"][:, 0]])),
        "cst": cst, "sel": sel, "par": par,
        "w_dt": w_in[:, PROJ * P:].reshape(KD, P, NH).transpose(1, 0, 2),
        "w_ring": np.concatenate([tiles(w_in[:, :PROJ * P]).reshape(N_IN, P, D), w_out,
                                  tiles(x["peer_wq"][0]).reshape(N_Q, P, D)]),
        "keys": x["peer_keys"][0].reshape(2 * PH, NKEY, P).transpose(2, 0, 1),
        "state_conv": x["state_conv"][0].reshape(NB, CONV_W - 1, CONV_CH, P).transpose(3, 2, 0, 1),
        "state_ssm": x["state_ssm"][0].reshape(NB, KD, P, P).transpose(2, 1, 0, 3),
        "page_table": x["page_table"].astype(np.int32).reshape(1, -1),
        "cache_k": x["cache_k"][0].reshape(n_pool, PAGE, KD, P).transpose(0, 3, 2, 1).reshape(n_pool, P, D),
        "cache_v": x["cache_v"][0].reshape(n_pool, PAGE, D),
        "uv": np.concatenate([
            x["peer_u"][0].reshape(NKEY, P, 2, KD // 2, P).transpose(0, 2, 4, 3, 1).reshape(-1, P, PIECE),
            x["peer_v"][0].reshape(NG, GRP, P, KD, P).transpose(0, 3, 2, 1, 4).reshape(-1, P, PIECE)]),
    }
    outs = {"y_out": (P, KD, NT), "k_out": (P, KD, NT), "v_out": (P, KD, NT), "conv_p": (P, CONV_CH, CONV_W - 1),
            "conv_s": (P, CONV_CH, NB, CONV_W - 1), "ssm_p": (P, KD, P), "ssm_s": (P, KD, NB, P)}
    nc = _bacc.Bacc("TRN2", target_bir_lowering=False, num_devices=1)
    t = {"n_pool": n_pool}
    arrays = {}
    for name, a in ins.items():
        a = np.ascontiguousarray(a)
        arrays[f"in_{name}"] = a
        t[name] = nc.dram_tensor(f"in_{name}", a.shape, mybir.dt.from_np(a.dtype), kind="ExternalInput").ap()
    for name, shape in outs.items():
        t[name] = nc.dram_tensor(f"out_{name}", shape, F32, kind="ExternalOutput").ap()
    build(nc, t)
    r = _run(nc, [arrays], core_ids=[0]).results[0]
    tok = {n: np.asarray(r[f"out_{n}"]).transpose(2, 1, 0).reshape(NT, D) for n in ("y_out", "k_out", "v_out")}
    heads = lambda a: (a[:TP].reshape(1, 1, TP, NH, HD), a[TP:].reshape(1, NB, 1, NH, HD))
    k_p, k_s = heads(tok["k_out"])
    v_p, v_s = heads(tok["v_out"])
    conv_p = np.asarray(r["out_conv_p"]).transpose(2, 1, 0).reshape(1, 1, CONV_W - 1, -1)
    conv_s = np.asarray(r["out_conv_s"]).transpose(2, 3, 1, 0).reshape(1, NB, CONV_W - 1, -1)
    ssm_p = np.asarray(r["out_ssm_p"]).transpose(1, 2, 0).reshape(1, 1, NH, HD, P)
    ssm_s = np.asarray(r["out_ssm_s"]).transpose(2, 1, 0, 3).reshape(1, NB, NH, HD, P)
    c = np.ascontiguousarray
    return (c(tok["y_out"][:TP].reshape(1, TP, D)), c(tok["y_out"][TP:].reshape(NB, 1, D)), c(k_p), c(v_p), c(k_s), c(v_s),
            c(conv_p), c(conv_s), c(ssm_p), c(ssm_s))
```
